# Optimizing a Trainium2 kernel written in Bass

```python
import jax, jax.numpy as jnp
from jax import lax
import numpy as np

D_MODEL = 1024
BATCH = 1
SEQ = 512
DEPTH = 2

CHUNK = 64
Q_BLOCK = 128
PLE_DIM = 256
EPS = 1e-6
NEG_INF = -1e30

SGU_WIDTH = 512
SGU_GROUPS = 4
SGU_GROUP_DIM = SGU_WIDTH // SGU_GROUPS
SGU_BLOCK = 128
POOL_WINDOWS = (2, 4, 8, 16)
POOL_WIDTH = 512
POOL_GROUPS = len(POOL_WINDOWS)
POOL_GROUP_DIM = POOL_WIDTH // POOL_GROUPS
MLA_HEADS = 4
MLA_NOPE = 128
MLA_ROPE = 64
MLA_QK = MLA_NOPE + MLA_ROPE
MLA_V = 128
MLA_WIDTH = MLA_HEADS * MLA_V
MLA_Q_RANK = 256
MLA_KV_RANK = 128
ROPE_THETA = 10000.0
SB_HEADS = 4
SB_HEAD_DIM = 128
SB_WIDTH = SB_HEADS * SB_HEAD_DIM

N_BRANCH = 4
IN_SIZES = (SGU_WIDTH, SGU_WIDTH, SGU_WIDTH,
            POOL_WIDTH, POOL_WIDTH,
            MLA_Q_RANK, MLA_KV_RANK, MLA_ROPE, MLA_WIDTH,
            SB_WIDTH, SB_WIDTH, SB_WIDTH, SB_WIDTH,
            N_BRANCH * D_MODEL)
N_IN = sum(IN_SIZES)

kernel_name = 'hybrid_gated_parallel_streaming_block'

def rms_norm(x, g):
    xf = x.astype(jnp.float32)
    y = xf * lax.rsqrt(jnp.mean(xf * xf, axis=-1, keepdims=True) + EPS)
    return (y * g.astype(jnp.float32)).astype(x.dtype)

def layer_norm(x, g, b):
    xf = x.astype(jnp.float32)
    mu = jnp.mean(xf, axis=-1, keepdims=True)
    xc = xf - mu
    y = xc * lax.rsqrt(jnp.mean(xc * xc, axis=-1, keepdims=True) + EPS)
    return (y * g.astype(jnp.float32) + b.astype(jnp.float32)).astype(x.dtype)

def apply_rope(x, positions):
    half = x.shape[-1] // 2
    freqs = ROPE_THETA ** (-jnp.arange(half, dtype=jnp.float32) / half)
    ang = positions.astype(jnp.float32)[:, :, None] * freqs
    cos = jnp.cos(ang)[:, :, None, :]
    sin = jnp.sin(ang)[:, :, None, :]
    xf = x.astype(jnp.float32)
    x1, x2 = xf[..., :half], xf[..., half:]
    return jnp.concatenate([x1 * cos - x2 * sin, x2 * cos + x1 * sin], axis=-1).astype(x.dtype)

def sweep_query_blocks(block_fn, q):
    b, s, h, d = q.shape
    nb = s // Q_BLOCK
    qb = q.reshape(b, nb, Q_BLOCK, h, d).transpose(1, 0, 2, 3, 4)
    out = lax.map(block_fn, (qb, jnp.arange(nb)))
    return out.transpose(1, 0, 2, 3, 4).reshape(b, s, h, out.shape[-1])

def spatial_gating(u, v, ln_g, ln_b, w_s, b_s):
    b, s, _ = v.shape
    v = layer_norm(v, ln_g, ln_b)
    nb = s // SGU_BLOCK
    vb = v.reshape(b, nb, SGU_BLOCK, SGU_GROUPS, SGU_GROUP_DIM)
    pos_chunk = jnp.arange(SGU_BLOCK) // CHUNK
    mask = pos_chunk[None, :] <= pos_chunk[:, None]
    w = jnp.where(mask[None], w_s, jnp.zeros_like(w_s))
    mixed = jnp.einsum('gts,bnsgc->bntgc', w, vb) + b_s.T[None, None, :, :, None]
    return u * mixed.reshape(b, s, SGU_WIDTH)

def multiscale_pool(xb, w_pool, scale):
    b, s, _ = xb.shape
    xf = xb.astype(jnp.float32).reshape(b, s, POOL_GROUPS, POOL_GROUP_DIM)
    cs = jnp.cumsum(xf, axis=1)
    t = jnp.arange(s)
    pooled = []
    for g, win in enumerate(POOL_WINDOWS):
        csg = cs[:, :, g]
        lagged = jnp.pad(csg, ((0, 0), (win, 0), (0, 0)))[:, :s]
        count = jnp.minimum(t + 1, win).astype(jnp.float32)[None, :, None]
        pooled.append((csg - lagged) / count - xf[:, :, g])
    pooled = jnp.stack(pooled, axis=2)
    y = jnp.einsum('bsgc,gcd->bsgd', pooled, w_pool.astype(jnp.float32)).reshape(b, s, POOL_WIDTH)
    return (y * scale.astype(jnp.float32)).astype(xb.dtype)

def latent_attention(c_q, c_kv, c_kr, positions, cq_g, w_uq, ckv_g, w_ukv, qn_g, kn_g):
    b, s, _ = c_q.shape
    q = (rms_norm(c_q, cq_g) @ w_uq).reshape(b, s, MLA_HEADS, MLA_QK)
    kv = (rms_norm(c_kv, ckv_g) @ w_ukv).reshape(b, s, MLA_HEADS, MLA_NOPE + MLA_V)
    k_nope, v = kv[..., :MLA_NOPE], kv[..., MLA_NOPE:]
    k_rope = jnp.broadcast_to(c_kr[:, :, None, :], (b, s, MLA_HEADS, MLA_ROPE))
    k = jnp.concatenate([k_nope, k_rope], axis=-1)
    q = rms_norm(q, qn_g)
    k = rms_norm(k, kn_g)
    q = jnp.concatenate([q[..., :MLA_NOPE], apply_rope(q[..., MLA_NOPE:], positions)], axis=-1)
    k = jnp.concatenate([k[..., :MLA_NOPE], apply_rope(k[..., MLA_NOPE:], positions)], axis=-1)
    qf, kf, vf = q.astype(jnp.float32), k.astype(jnp.float32), v.astype(jnp.float32)
    key_chunk = jnp.arange(s) // CHUNK
    scale = MLA_QK ** -0.5

    def block(args):
        qi, i = args
        sc = jnp.einsum('bqhd,bkhd->bhqk', qi, kf) * scale
        q_chunk = (i * Q_BLOCK + jnp.arange(Q_BLOCK)) // CHUNK
        mask = key_chunk[None, :] <= q_chunk[:, None]
        w = jax.nn.softmax(jnp.where(mask, sc, NEG_INF), axis=-1)
        return jnp.einsum('bhqk,bkhd->bqhd', w, vf)

    o = sweep_query_blocks(block, qf)
    return o.reshape(b, s, MLA_WIDTH).astype(c_q.dtype)

def stick_breaking_attention(q, k, v):
    b, s, _ = q.shape
    qf = q.astype(jnp.float32).reshape(b, s, SB_HEADS, SB_HEAD_DIM)
    kf = k.astype(jnp.float32).reshape(b, s, SB_HEADS, SB_HEAD_DIM)
    vf = v.astype(jnp.float32).reshape(b, s, SB_HEADS, SB_HEAD_DIM)
    key_pos = jnp.arange(s)
    scale = SB_HEAD_DIM ** -0.5

    def block(args):
        qi, i = args
        z = jnp.einsum('bqhd,bkhd->bhqk', qi, kf) * scale
        q_pos = i * Q_BLOCK + jnp.arange(Q_BLOCK)
        strict = key_pos[None, :] < q_pos[:, None]
        log_keep = jnp.where(strict, jax.nn.log_sigmoid(-z), 0.0)
        after = lax.cumsum(log_keep, axis=3, reverse=True) - log_keep
        a = jnp.where(strict, jnp.exp(jax.nn.log_sigmoid(z) + after), 0.0)
        return jnp.einsum('bhqk,bkhd->bqhd', a, vf)

    o = sweep_query_blocks(block, qf)
    return o.reshape(b, s, SB_WIDTH).astype(q.dtype)

def setup_inputs(seed: int = 0) -> dict:
    key = jax.random.key(seed)
    ks = jax.random.split(key, 32)
    f32 = jnp.float32

    def nrm(k, shape, scale):
        return jax.random.normal(k, shape, f32) * scale

    def gain(k, shape):
        return 1.0 + 0.05 * jax.random.normal(k, shape, f32)

    x = jax.random.normal(ks[0], (BATCH, SEQ, D_MODEL), f32)
    p = jax.random.normal(ks[1], (DEPTH, BATCH, SEQ, PLE_DIM), f32)
    offsets = jax.random.randint(ks[2], (BATCH, 1), 0, 4096, dtype=jnp.int32)
    positions = (jnp.arange(SEQ, dtype=jnp.int32)[None, :] + offsets).astype(jnp.int32)
    return {
        'x': x,
        'p': p,
        'positions': positions,
        'norm_g': gain(ks[3], (DEPTH, D_MODEL)),
        'w_in': nrm(ks[4], (DEPTH, D_MODEL, N_IN), D_MODEL ** -0.5),
        'ln_v_g': gain(ks[5], (DEPTH, SGU_WIDTH)),
        'ln_v_b': nrm(ks[6], (DEPTH, SGU_WIDTH), 0.02),
        'sgu_w': nrm(ks[7], (DEPTH, SGU_GROUPS, SGU_BLOCK, SGU_BLOCK), SGU_BLOCK ** -0.5),
        'sgu_b': 1.0 + 0.1 * jax.random.normal(ks[8], (DEPTH, SGU_GROUPS, SGU_BLOCK), f32),
        'w_a_out': nrm(ks[9], (DEPTH, SGU_WIDTH, D_MODEL), SGU_WIDTH ** -0.5),
        'pool_w': nrm(ks[10], (DEPTH, POOL_GROUPS, POOL_GROUP_DIM, POOL_GROUP_DIM), POOL_GROUP_DIM ** -0.5),
        'pool_scale': 1.0 + 0.1 * jax.random.normal(ks[11], (DEPTH, POOL_WIDTH), f32),
        'w_b_out': nrm(ks[12], (DEPTH, POOL_WIDTH, D_MODEL), POOL_WIDTH ** -0.5),
        'cq_norm_g': gain(ks[13], (DEPTH, MLA_Q_RANK)),
        'w_uq': nrm(ks[14], (DEPTH, MLA_Q_RANK, MLA_HEADS * MLA_QK), MLA_Q_RANK ** -0.5),
        'ckv_norm_g': gain(ks[15], (DEPTH, MLA_KV_RANK)),
        'w_ukv': nrm(ks[16], (DEPTH, MLA_KV_RANK, MLA_HEADS * (MLA_NOPE + MLA_V)), MLA_KV_RANK ** -0.5),
        'q_norm_g': gain(ks[17], (DEPTH, MLA_QK)),
        'k_norm_g': gain(ks[18], (DEPTH, MLA_QK)),
        'w_c_out': nrm(ks[19], (DEPTH, MLA_WIDTH, D_MODEL), MLA_WIDTH ** -0.5),
        'w_d_out': nrm(ks[20], (DEPTH, SB_WIDTH, D_MODEL), SB_WIDTH ** -0.5),
        'w_o': nrm(ks[21], (DEPTH, D_MODEL, D_MODEL), D_MODEL ** -0.5),
        'w_ple': nrm(ks[22], (DEPTH, PLE_DIM, D_MODEL), PLE_DIM ** -0.5),
        'ple_norm_g': gain(ks[23], (DEPTH, D_MODEL)),
        'w_ple_gate': nrm(ks[24], (DEPTH, D_MODEL, D_MODEL), D_MODEL ** -0.5),
    }

def reference(x, p, positions, norm_g, w_in, ln_v_g, ln_v_b, sgu_w, sgu_b, w_a_out,
              pool_w, pool_scale, w_b_out, cq_norm_g, w_uq, ckv_norm_g, w_ukv,
              q_norm_g, k_norm_g, w_c_out, w_d_out, w_o, w_ple, ple_norm_g, w_ple_gate):
    b, s, d = x.shape
    split_at = [int(o) for o in np.cumsum(IN_SIZES)[:-1]]
    for i in range(DEPTH):
        h = rms_norm(x, norm_g[i])
        proj = h @ w_in[i]
        (a_u, a_v, a_z, b_x, b_z, c_q, c_kv, c_kr, c_z,
         d_q, d_k, d_v, d_z, gates) = jnp.split(proj, split_at, axis=-1)

        y_a = (spatial_gating(a_u, a_v, ln_v_g[i], ln_v_b[i], sgu_w[i], sgu_b[i])
               * jax.nn.silu(a_z)) @ w_a_out[i]
        y_b = (multiscale_pool(b_x, pool_w[i], pool_scale[i]) * jax.nn.silu(b_z)) @ w_b_out[i]
        y_c = (latent_attention(c_q, c_kv, c_kr, positions, cq_norm_g[i], w_uq[i],
                                ckv_norm_g[i], w_ukv[i], q_norm_g[i], k_norm_g[i])
               * jax.nn.silu(c_z)) @ w_c_out[i]
        y_d = (stick_breaking_attention(d_q, d_k, d_v) * jax.nn.silu(d_z)) @ w_d_out[i]

        g = jax.nn.sigmoid(gates).reshape(b, s, N_BRANCH, d)
        branches = jnp.stack([y_a, y_b, y_c, y_d], axis=2)
        merged = jnp.sum(g * branches, axis=2)
        x = x + merged @ w_o[i]

        e = p[i] @ w_ple[i]
        x = x + jax.nn.sigmoid(rms_norm(x, ple_norm_g[i]) @ w_ple_gate[i]) * e
    return x


_drawn_inputs = setup_inputs


def setup_inputs(seed=0):
    import zlib

    import numpy as np

    out = dict(_drawn_inputs(seed))
    spreads = {}
    factors = {'ln_v_g': 3.481,
     'ln_v_b': 8.0,
     'cq_norm_g': 8.0,
     'ckv_norm_g': 8.0,
     'q_norm_g': 8.0,
     'k_norm_g': 8.0,
     'ple_norm_g': 5.072}
    for name, (base, spread) in spreads.items():
        noise = np.random.default_rng([zlib.crc32(name.encode()), seed]).standard_normal(out[name].shape)
        drawn = base * np.exp(spread * noise) if base else spread * noise
        out[name] = __import__('jax').numpy.asarray(drawn.astype(out[name].dtype))
    for name, factor in factors.items():
        out[name] = (out[name] * factor).astype(out[name].dtype)
    return out
```

```python
from contextlib import ExitStack

import numpy as np

import concourse.bass as bass
from concourse import mybir

F32 = mybir.dt.float32
F32R = mybir.dt.float32r
BF16 = mybir.dt.bfloat16
I32 = mybir.dt.int32
ALU = mybir.AluOpType
ACT = mybir.ActivationFunctionType

P = 128
D_MODEL, SEQ, DEPTH = 1024, 512, 2
KD = D_MODEL // P
TB = SEQ // P
G = 4
PLE = 256
ROPE = 64
QK = P + ROPE
EPS = 1e-6
NEG = -1e30
Q_SCALE_C = QK ** -0.5
Q_SCALE_D = P ** -0.5
PAD = 16

A_U, A_V, A_Z, B_X, B_Z = 0, 512, 1024, 1536, 2048
C_Q, C_KV, C_KR, C_Z = 2560, 2816, 2944, 3008
D_Q, D_K, D_V, D_Z, GATES = 3520, 4032, 4544, 5056, 5568

J_LAT = 0
J_AV = 4
J_H1 = J_AV + G
J_M1 = J_H1 + 4 * G
J_MIX = J_M1 + 3 * KD
J_H2 = J_MIX + 1
J_M2 = J_H2 + 6 * G
J_WO = J_M2 + 3 * KD
J_PLE = J_WO + KD
J_GATE = J_PLE + 2
CHUNKS = J_GATE + KD
RING = 4
CREDIT = RING
SLOT_USES = [len(range(s, CHUNKS, RING)) for s in range(RING)]

W_QN, W_QR, W_KN, W_V, W_POOL = 0, 2, 4, 5, 6

def columns(*parts):
    made, at = {}, 0
    for name, width in parts:
        made[name] = slice(at, at + width)
        at += width
    return made, at


PC, PARAMS = columns(("norm", KD), ("ple", KD), ("pool", G), ("cq", 2), ("ckv", 1), ("qn", 1), ("qr", 1),
                     ("kn", 1), ("kr", 1))
CC, CONSTS = columns(("ident", P), ("ones", P), ("negtri", P), ("neg_i", P), ("mask_c", P), ("mask_d", P),
                     ("inv_edge", G * PAD), ("inv_win", G), ("freq", 1))

ROW_AT = {3: 0, 2: 512, 0: 896, 1: 1024}
COL_AT = {0: 0, 1: 512, 3: 896, 2: 1024}
TRI = 1280


TWO_PI = (6.28125, 0.0019350051879882812, 3.019916050561733e-07)
PI_IN = 3.1415925
ROUND = 12582912.0

STEPS = dict(start=12, norm=2, latents=16, half1=33, ln=27, merge0=8, merge1=20, half2=20, out=2)


def nth(l, quads, j):
    return l * CHUNKS + quads * RING + j




def after(n):
    return n + (1 + CREDIT)


class Steps:

    def __init__(self, done, base, per):
        self.done, self.base, self.per, self.n = done, base, per, 0

    def next(self):
        self.n += 1
        return self.base + self.n

    def close(self):
        assert self.n == self.per, f"{self.n} steps, not {self.per}"


def build(nc, x_in, p_in, pos_in, w_in, par_in, rows_in, const_in, out):
    ctx = ExitStack()
    with ctx:
        def sb(name, shape, dt=F32):
            return ctx.enter_context(nc.sbuf_tensor(name, shape, dt))

        x = sb("x", [P, KD * SEQ])
        h_hi = sb("h_hi", [P, KD * SEQ], F32R)
        h_lo = sb("h_lo", [P, KD * SEQ], F32R)
        act_hi = sb("act_hi", [P, 2 * G * SEQ], F32R)
        act_lo = sb("act_lo", [P, 2 * G * SEQ], F32R)
        w_hi_t = [sb(f"w_hi{s}", [P, 8, P], F32R) for s in range(RING)]
        ident = sb("ident", [P, P])
        ones = sb("ones", [P, P])
        negtri = sb("negtri", [P, P], F32R)
        negones = sb("negones", [P, P], F32R)
        neg_i = sb("neg_i", [P, P], BF16)
        mask_c = sb("mask_c", [P, P], BF16)
        mask_d = sb("mask_d", [P, P], BF16)
        inv_edge = sb("inv_edge", [P, G * PAD])
        inv_win = sb("inv_win", [P, G])
        cos_t = sb("cos_t", [P, SEQ])
        sin_t = sb("sin_t", [P, SEQ])
        par_all = sb("par_all", [P, DEPTH * PARAMS])
        par = sb("par", [P, PARAMS])
        small = sb("small", [P, 32])
        edge = sb("edge", [P, PAD])
        eps = sb("eps", [P, 1])

        ring_at = (nc.sbuf_base + 31) // 32 * 32
        CH = 8 * P * 4
        ARENA = 88 * 1024
        sb("arena", [P, (RING * CH + ARENA) // 4])
        arena_at = ring_at + RING * CH

        def at(name, offset, shape, dt=F32, base=arena_at):
            return nc.alloc_sbuf_tensor_at(name, shape, dt, offset=base + offset)

        w_raw_t = [at(f"w_raw{s}", s * CH, [P, 8, P], F32, ring_at) for s in range(RING)]
        w_lo_t = [at(f"w_lo{s}", s * CH, [P, 8, P], F32R, ring_at) for s in range(RING)]

        K = 1024

        def plan(start, *items):
            made, o = [], start
            for name, shape, dt in items:
                made.append(at(name, o, [P, *shape], dt))
                o += -(-int(np.prod(shape)) * 4 // 32) * 32
            assert o <= ARENA, (items, o)
            return made

        cqn_hi, cqn_lo, ckvn_hi, ckvn_lo, krr, sq_kr = plan(
            0, ("cqn_hi", [2, SEQ], F32R), ("cqn_lo", [2, SEQ], F32R), ("ckvn_hi", [SEQ], F32R),
            ("ckvn_lo", [SEQ], F32R), ("krr", [SEQ], F32), ("sq_kr", [SEQ], F32))
        (qn_hi, qn_lo, qr_hi, qr_lo, kn_hi, kn_lo, kr_hi, kr_lo, cv_hi, cv_lo, sq_a, sq_b, sq_k, tmp0, tmp1, r_k,
         prob, pt_hi, pt_lo, sz_c, bx, cs_pad, diff, pool_hi, pool_lo, sz_b) = plan(
            16 * K,
            *[(n, [SEQ], F32R) for n in ("qn_hi", "qn_lo", "qr_hi", "qr_lo", "kn_hi", "kn_lo", "kr_hi", "kr_lo",
                                         "cv_hi", "cv_lo")],
            *[(n, [SEQ], F32) for n in ("sq_a", "sq_b", "sq_k", "tmp0", "tmp1", "r_k")],
            ("prob", [TRI], F32), ("pt_hi", [TRI], F32R), ("pt_lo", [TRI], F32R),
            ("sz_c", [SEQ], F32), ("bx", [SEQ], F32), ("cs_pad", [SEQ + PAD], F32),
            ("diff", [SEQ], F32), ("pool_hi", [SEQ], F32R), ("pool_lo", [SEQ], F32R), ("sz_b", [SEQ], F32))
        n_sq, n_t = plan(16 * K, ("n_sq", [2, SEQ], F32), ("n_t", [2, SEQ], F32))
        n_acc, n_r = plan(24 * K, ("n_acc", [SEQ], F32), ("n_r", [SEQ], F32))
        (av_t,) = plan(80 * K, ("av_t", [G * SEQ], F32))
        (mix_t,) = plan(80 * K, ("mix_t", [G * SEQ], F32))
        (merged,) = plan(0, ("merged", [KD * SEQ], F32))
        m_hi, m_lo = plan(16 * K, ("m_hi", [KD * SEQ], F32R), ("m_lo", [KD * SEQ], F32R))
        th, m_part = plan(48 * K, ("th", [4, SEQ], F32), ("m_part", [2, SEQ], F32))
        rows, xh = plan(28 * K, ("rows", [3, SEQ], F32), ("xh", [SEQ], F32))
        vn_hi, vn_lo = plan(60 * K, ("vn_hi", [TB * SEQ], F32R), ("vn_lo", [TB * SEQ], F32R))
        (dq_hi, dq_lo, dk_hi, dk_lo, dv_t, dv_hi, dv_lo, z_s, sp, s_hi, s_lo, a_u, sz_a, sz_d, tmp2) = plan(
            16 * K,
            *[(n, [SEQ], F32R) for n in ("dq_hi", "dq_lo", "dk_hi", "dk_lo")], ("dv_t", [SEQ], F32),
            *[(n, [SEQ], F32R) for n in ("dv_hi", "dv_lo")],
            ("z_s", [TRI], F32), ("sp", [TRI], F32), ("s_hi", [TRI], F32R), ("s_lo", [TRI], F32R),
            *[(n, [SEQ], F32) for n in ("a_u", "sz_a", "sz_d", "tmp2")])
        p_raw, p_hi, p_lo, e = plan(60 * K, ("p_raw", [2, SEQ], F32), ("p_hi", [2, SEQ], F32R),
                                    ("p_lo", [2, SEQ], F32R), ("e", [KD * SEQ], F32))
        o_acc, o_sq, o_r, o_t = plan(48 * K, ("o_acc", [SEQ], F32), ("o_sq", [2, SEQ], F32), ("o_r", [SEQ], F32),
                                     ("o_t", [2, SEQ], F32))
        c_st, pos_i, ang, turns = plan(0, ("c_st", [CONSTS], F32), ("pos_i", [SEQ], I32), ("ang", [SEQ], F32),
                                       ("turns", [SEQ], F32))

        ps = ctx.enter_context(nc.psum_tensor("ps", [P, 8 * 512], F32))

        def bank(b, n=512):
            return ps[:, b * 512:b * 512 + n]

        SC = 2 * 512
        PTB = 5 * 512

        given = {"pe": [], "act": [], "dve": [], "pool": []}

        def sem(name):
            return ctx.enter_context(nc.semaphore(name))

        def signals(engine, names):
            made = [sem(n) for n in names.split()]
            given[engine] += made
            return made if len(made) > 1 else made[0]

        x_loaded, pos_loaded = sem("x_loaded"), sem("pos_loaded")
        par_loaded, const_loaded = sem("par_loaded"), sem("const_loaded")
        rows_loaded, p_loaded, out_stored = sem("rows_loaded"), sem("p_loaded"), sem("out_stored")
        raw_loaded = [sem(f"raw_loaded{s}") for s in range(RING)]
        w_hi_made = signals("act", "w_hi_made")
        w_lo_made = signals("pool", "w_lo_made")
        chunk_done = signals("pe", "chunk_done")
        consts_made, rope_args, n_scaled, h_made = signals(
            "dve", "consts_made rope_args n_scaled h_made")
        n_sq_used = signals("dve", "n_sq_used")
        rope_sines, n_squared, n_root, n_hi_made = signals("act", "rope_sines n_squared n_root n_hi_made")
        n_total = signals("pe", "n_total")
        lat_total = signals("pe", "lat_total")
        lat_squared, lat_root = signals("act", "lat_squared lat_root")
        av_taken = signals("act", "av_taken")
        lat_summed, lat_made = signals("dve", "lat_summed lat_made")
        c_ready, stat_ready, s_ready, pt_ready, oc_ready = signals("pe", "c_ready stat_ready s_ready pt_ready oc_ready")
        c_squared, cv_hi_made, c_root, exp_made, pt_hi_made, cz_tanh, bz_tanh = signals(
            "act", "c_squared cv_hi_made c_root exp_made pt_hi_made cz_tanh bz_tanh")
        (bx_taken, pooled, q_made, sqk_made, cv_made, pool_taken, k_made, s_max, p_made, pt_made, cz_taken, bz_taken,
         act1_made) = signals(
            "dve", "bx_taken pooled q_made sqk_made cv_made pool_taken k_made s_max p_made pt_made cz_taken bz_taken "
                   "act1_made")
        ln_ready, mix_ready, y_ready = signals("pe", "ln_ready mix_ready y_ready")
        ln_root, g_tanh = signals("act", "ln_root g_tanh")
        ln_var, ln_made, wt_masked, mix_taken = signals("dve", "ln_var ln_made wt_masked mix_taken")
        m_done = signals("dve", "m_done")
        z_ready, dvt_ready, cum_ready, od_ready = signals("pe", "z_ready dvt_ready cum_ready od_ready")
        dv_taken, dk_hi_made, dv_hi_made, z_log, a_made, au_taken, az_tanh, dz_tanh = signals(
            "act", "dv_taken dk_hi_made dv_hi_made z_log a_made au_taken az_tanh dz_tanh")
        dq_made, dk_made, sp_made, dv_made, a_split, az_taken, dz_taken, act2_made = signals(
            "dve", "dq_made dk_made sp_made dv_made a_split az_taken dz_taken act2_made")
        e_ready, o_total = signals("pe", "e_ready o_total")
        o_squared, o_root, gate_tanh = signals("act", "o_squared o_root gate_tanh")
        e_taken = signals("act", "e_taken")
        p_split, hx_hi, hx_made, o_inv, gated = signals("dve", "p_split hx_hi hx_made o_inv gated")
        x_moved, x_made, o_summed, gate_scaled = signals("dve", "x_moved x_made o_summed gate_scaled")
        act_steps = sem("act_steps")
        own = {k: sem(f"dve_steps_{k}") for k in STEPS}

        block = ctx.enter_context(nc.Block())

        def tile(t, i, n=SEQ):
            return t[:, bass.ds(i * n, n)] if not isinstance(i, int) else t[:, i * n:(i + 1) * n]

        @block.sync
        def _(sync):
            def load(l, quads, j, before):
                s = j % RING
                sync.wait_ge(chunk_done, after(l * CHUNKS + quads * RING + (before - 1)))
                sync.dma_start(w_raw_t[s][:], w_in[l * CHUNKS + quads * RING + j]).then_inc(raw_loaded[s], 16)

            sync.dma_start(x[:], x_in).then_inc(x_loaded, 16)
            sync.dma_start(c_st[:], const_in).then_inc(const_loaded, 16)
            sync.dma_start(par_all[:], par_in).then_inc(par_loaded, 16)
            sync.dma_start(pos_i[:], pos_in.partition_broadcast(P)).then_inc(pos_loaded, 16)
            with sync.Fori(0, DEPTH) as l:
                for j in range(RING):
                    load(l, 0, j, (CHUNKS - 1 - j) // RING * RING + j + 1 - CHUNKS)
                full = CHUNKS // RING
                with sync.Fori(1, full) as quads:
                    for j in range(RING):
                        load(l, quads, j, j + 1 - RING)
                for j in range(RING * full, CHUNKS):
                    load(l, 0, j, j + 1 - RING)
            for d in range(KD):
                sync.wait_ge(x_made, after((DEPTH - 1) * KD + d))
                sync.dma_start(out[:, d * SEQ:(d + 1) * SEQ], tile(x, d)).then_inc(out_stored, 16)
            sync.wait_ge(out_stored, 16 * KD)

        @block.gpsimd
        def _(pool):
            for s in given["pool"]:
                pool.sem_inc(s, CREDIT)

            def lo(l, quads, j):
                s = j % RING
                pool.wait_ge(w_hi_made, after(nth(l, quads, j)))
                pool.tensor_tensor(w_lo_t[s][:], w_raw_t[s][:], w_hi_t[s][:].bitcast(F32),
                                   ALU.subtract).then_inc(w_lo_made, 1)

            with pool.Fori(0, DEPTH) as l:
                full = CHUNKS // RING
                with pool.Fori(0, full) as quads:
                    for j in range(RING):
                        lo(l, quads, j)
                for j in range(RING * full, CHUNKS):
                    lo(l, 0, j)

        @block.tensor
        def _(pe):
            for s in given["pe"]:
                pe.sem_inc(s, CREDIT)

            def chunk(l, quads, j):
                pe.wait_ge(w_lo_made, after(nth(l, quads, j)))
                return w_hi_t[j % RING], w_lo_t[j % RING]

            def mm3(o, a_hi, a_lo, b_hi, b_lo, first=True, last=True, skip=False):
                pe.matmul(o, a_hi, b_hi, start=first, stop=False, skip_group_check=skip)
                pe.matmul(o, a_hi, b_lo, start=False, stop=False, skip_group_check=skip)
                return pe.matmul(o, a_lo, b_hi, start=False, stop=last, skip_group_check=skip)

            def project_k(w, o, k):
                return mm3(o, w[0][:, k, :], w[1][:, k, :], tile(h_hi, k), tile(h_lo, k), k == 0, k == KD - 1)

            def project(l, quads, j, b):
                w = chunk(l, quads, j)
                for k in range(KD):
                    last = project_k(w, bank(b), k)
                last.then_inc(chunk_done, 1)

            pe.wait_ge(consts_made, after(0))
            with pe.Fori(0, DEPTH) as l:
                pe.wait_ge(n_sq_used, after(l * KD + (KD - 1)))
                pe.matmul(bank(7), ones[:], n_acc[:], start=True, stop=True).then_inc(n_total, 1)

                w0, w1 = chunk(l, 0, J_LAT), chunk(l, 0, J_LAT + 1)
                for k in range(KD):
                    pe.wait_ge(h_made, after(l * KD + k))
                    last0 = project_k(w0, bank(0), k)
                    last1 = project_k(w1, bank(1), k)
                last0.then_inc(chunk_done, 1)
                last1.then_inc(chunk_done, 1)
                project(l, 0, J_LAT + 2, 2)
                project(l, 0, J_LAT + 3, 3)
                for g in range(G):
                    if g >= 2:
                        pe.wait_ge(av_taken, after(l * G + (g - 2)))
                    project(l, 0, J_AV + g, 6 + g % 2)
                    if g == 0:
                        pe.wait_ge(lat_summed, after(l))
                        pe.matmul(bank(4), ones[:], sq_a[:], start=True, stop=True).then_inc(lat_total, 1)
                        pe.wait_ge(lat_squared, after(l * 4 + 3))
                        pe.matmul(bank(5), ones[:], tmp1[:], start=True, stop=True).then_inc(lat_total, 1)

                latents, values = pe.to_reg(after(l)), pe.to_reg(after(l * G + (G - 1)))
                pe.wait_ge(const_loaded, 16)
                pe.wait_ge(lat_made, latents)
                pe.wait_ge(av_taken, values)
                with pe.Fori(0, G) as g:
                    n = l * G + g
                    pe.wait_ge(cz_taken, after(n - 1))
                    project(l, g, J_H1, 0)

                    w_hi, w_lo = chunk(l, g, J_H1 + 1)
                    for b, at_, q in ((4, W_QN, True), (5, W_QR, True), (6, W_KN, False)):
                        if q:
                            mm3(bank(b), w_hi[:, at_, :], w_lo[:, at_, :], cqn_hi[:, 0, :], cqn_lo[:, 0, :], True, False)
                            last = mm3(bank(b), w_hi[:, at_ + 1, :], w_lo[:, at_ + 1, :], cqn_hi[:, 1, :],
                                       cqn_lo[:, 1, :], False, True)
                        else:
                            last = mm3(bank(b), w_hi[:, at_, :], w_lo[:, at_, :], ckvn_hi[:], ckvn_lo[:])
                        last.then_inc(c_ready, 1)
                    for t in range(TB):
                        last = mm3(ps[:, 7 * 512 + t * P:7 * 512 + (t + 1) * P], tile(ckvn_hi, t, P), tile(ckvn_lo, t, P),
                                   w_hi[:, W_V, :], w_lo[:, W_V, :])
                    last.then_inc(c_ready, 1)
                    pe.wait_ge(bz_taken, after(n - 1))
                    pe.wait_ge(pooled, after(n))
                    mm3(bank(1), w_hi[:, W_POOL, :], w_lo[:, W_POOL, :], pool_hi[:], pool_lo[:]).then_inc(
                        chunk_done, 1)

                    pe.wait_ge(bx_taken, after(n))
                    project(l, g, J_H1 + 2, 0)

                    pe.wait_ge(c_squared, after(n * 3 + 2))
                    for t in range(TB):
                        o = ps[:, 3 * 512 + t:3 * 512 + t + 1]
                        pe.matmul(o, tile(sq_a, t, P), ones[:, 0:1], start=True, stop=False)
                        last = pe.matmul(o, tile(sq_b, t, P), ones[:, 0:1], start=False, stop=True)
                    last.then_inc(stat_ready, 1)
                    pe.wait_ge(act1_made, after(n - 1))
                    pe.wait_ge(sqk_made, after(n))
                    pe.matmul(bank(2), ones[:], sq_k[:], start=True, stop=True).then_inc(stat_ready, 1)

                    pe.wait_ge(pool_taken, after(n))
                    project(l, g, J_H1 + 3, 1)

                    pe.wait_ge(q_made, after(n))
                    pe.wait_ge(k_made, after(n))
                    for b in (3, 2, 0, 1):
                        o = ps[:, SC + ROW_AT[b]:SC + ROW_AT[b] + (b + 1) * P]
                        keys = (b + 1) * P
                        mm3(o, tile(qn_hi, b, P), tile(qn_lo, b, P), kn_hi[:, 0:keys], kn_lo[:, 0:keys], b != 0,
                            False, True)
                        mm3(o, tile(qr_hi, b, P), tile(qr_lo, b, P), kr_hi[:, 0:keys], kr_lo[:, 0:keys], False,
                            False, True)
                        o = ps[:, SC + ROW_AT[b] + b * P:SC + ROW_AT[b] + (b + 1) * P]
                        last = pe.matmul(o, neg_i[:], mask_c[:], start=False, stop=True, skip_group_check=True)
                    last.then_inc(s_ready, 1)

                    pe.wait_ge(cv_made, after(n))
                    pe.wait_ge(p_made, after(n))
                    for kb in (0, 1, 3, 2):
                        for qb in range(kb, TB):
                            o = PTB + COL_AT[kb] + (qb - kb) * P
                            i = ROW_AT[qb] + kb * P
                            last = pe.transpose(ps[:, o:o + P], prob[:, i:i + P], ident[:])
                    last.then_inc(pt_ready, 1)
                    pe.wait_ge(pt_made, after(n))
                    for kb in range(TB):
                        c = slice(COL_AT[kb], COL_AT[kb] + SEQ - kb * P)
                        last = mm3(ps[:, 2 * 512 + kb * P:3 * 512], tile(cv_hi, kb, P), tile(cv_lo, kb, P),
                                   pt_hi[:, c], pt_lo[:, c], kb == 0, kb == TB - 1)
                    last.then_inc(oc_ready, 1)

                pe.wait_ge(act1_made, after(l * G + (G - 1)))
                for t in range(TB):
                    for g in range(G):
                        last = pe.transpose(ps[:, t * 512 + g * P:t * 512 + (g + 1) * P],
                                            av_t[:, g * SEQ + t * P:g * SEQ + (t + 1) * P], ident[:])
                    last.then_inc(ln_ready, 1)

                def merge(half, j_at):
                    with pe.Fori(0, 2) as i:
                        for u in range(4):
                            q = l * (2 * KD) + i * 4 + (half * KD + u)
                            b = 4 * (1 - u % 2)
                            pe.wait_ge(m_done, after(q - 2))
                            if half == 0 and u == 1:
                                pe.wait_ge(ln_made, after(l))
                            project(l, i * 3, j_at + 3 * u, b)
                            project(l, i * 3, j_at + 3 * u + 1, b + 1)
                            w_hi, w_lo = chunk(l, i * 3, j_at + 3 * u + 2)
                            if u == 0:
                                pe.wait_ge(act2_made if half else act1_made, after(l * G + (G - 1)))
                            for branch in range(2):
                                for k in range(G):
                                    last = mm3(bank(b + 2 + branch), w_hi[:, branch * G + k, :],
                                               w_lo[:, branch * G + k, :], tile(act_hi, branch * G + k),
                                               tile(act_lo, branch * G + k), k == 0, k == G - 1)
                                last.then_inc(chunk_done if branch else y_ready, 1)

                merge(0, J_M1)

                pe.wait_ge(m_done, after(l * (2 * KD) + (KD - 2)))
                w_hi, w_lo = chunk(l, 0, J_MIX)
                pe.wait_ge(wt_masked, after(l))
                for g in range(G):
                    for t in range(TB):
                        i = t * SEQ + g * P
                        last = mm3(ps[:, (4 + g) * 512 + t * P:(4 + g) * 512 + (t + 1) * P], vn_hi[:, i:i + P],
                                   vn_lo[:, i:i + P], w_hi[:, g, :], w_lo[:, g, :])
                    last.then_inc(mix_ready if g < G - 1 else chunk_done, 1)

                value = pe.to_reg(after(l * (2 * KD) + (KD - 1)))
                pe.wait_ge(const_loaded, 16)
                pe.wait_ge(m_done, value)
                with pe.Fori(0, 2) as i:
                    for u in range(2):
                        n = l * G + i * 2 + u
                        j = J_H2 + 6 * u
                        pe.wait_ge(az_taken, after(n - 1))
                        project(l, i * 3, j, 0)
                        pe.wait_ge(dz_taken, after(n - 1))
                        project(l, i * 3, j + 1, 1)
                        pe.wait_ge(dq_made, after(n))
                        project(l, i * 3, j + 2, 0)
                        if u == 0:
                            pe.wait_ge(mix_taken, after(l * G + (G - 1)))
                        pe.wait_ge(dk_made, after(n))
                        for kb in (0, 1, 3, 2):
                            c = SC + COL_AT[kb]
                            mm3(ps[:, c:c + SEQ - kb * P], tile(dk_hi, kb, P), tile(dk_lo, kb, P),
                                dq_hi[:, kb * P:SEQ], dq_lo[:, kb * P:SEQ], kb != 3, False, True)
                            last = pe.matmul(ps[:, c:c + P], neg_i[:], mask_d[:], start=False, stop=False,
                                             skip_group_check=True)
                        last.then_inc(z_ready, 1)
                        project(l, i * 3, j + 3, 1)
                        pe.wait_ge(dv_taken, after(n))
                        for t in range(TB):
                            last = pe.transpose(ps[:, 5 * 512 + t * P:5 * 512 + (t + 1) * P], tile(dv_t, t, P), ident[:])
                        last.then_inc(dvt_ready, 1)
                        pe.wait_ge(sp_made, after(n))
                        for kb in range(TB):
                            for jb in range(kb, TB):
                                c = SC + COL_AT[kb] + (jb - kb) * P
                                s = slice(COL_AT[jb], COL_AT[jb] + SEQ - jb * P)
                                o = ps[:, c:c + SEQ - jb * P]
                                m = negtri if jb == kb else negones
                                pe.matmul(o, m[:], s_hi[:, s], start=False, stop=False, skip_group_check=True)
                                last = pe.matmul(o, m[:], s_lo[:, s], start=False, stop=jb == TB - 1,
                                                 skip_group_check=True)
                        last.then_inc(cum_ready, 1)
                        project(l, i * 3, j + 4, 0)
                        pe.wait_ge(a_split, after(n))
                        pe.wait_ge(dv_made, after(n))
                        pe.wait_ge(act2_made, after(n - 1))
                        for kb in range(TB):
                            c = slice(COL_AT[kb], COL_AT[kb] + SEQ - kb * P)
                            last = mm3(ps[:, 6 * 512 + kb * P:7 * 512], tile(dv_hi, kb, P), tile(dv_lo, kb, P),
                                       s_hi[:, c], s_lo[:, c], kb == 0, kb == TB - 1)
                        last.then_inc(od_ready, 1)
                        pe.wait_ge(au_taken, after(n))
                        project(l, i * 3, j + 5, 1)

                merge(1, J_M2)

                value = pe.to_reg(after(l * (2 * KD) + (2 * KD - 1)))
                pe.wait_ge(const_loaded, 16)
                pe.wait_ge(m_done, value)
                with pe.Fori(0, 2) as i:
                    for u in range(4):
                        n = l * KD + i * 4 + u
                        pe.wait_ge(x_moved, after(n - 2))
                        w_hi, w_lo = chunk(l, i, J_WO + u)
                        for k in range(KD):
                            last = mm3(bank(u % 2), w_hi[:, k, :], w_lo[:, k, :], tile(m_hi, k), tile(m_lo, k), k == 0,
                                       k == KD - 1)
                        last.then_inc(chunk_done, 1)

                pe.wait_ge(p_split, after(l))
                for d in range(KD):
                    if d % 4 == 0:
                        w_hi, w_lo = chunk(l, 0, J_PLE + d // 4)
                    pe.wait_ge(e_taken, after(l * KD + (d - 2)))
                    mm3(bank(2 + d % 2), w_hi[:, d % 4 * 2, :], w_lo[:, d % 4 * 2, :], p_hi[:, 0, :], p_lo[:, 0, :],
                        True, False)
                    last = mm3(bank(2 + d % 2), w_hi[:, d % 4 * 2 + 1, :], w_lo[:, d % 4 * 2 + 1, :], p_hi[:, 1, :],
                               p_lo[:, 1, :], False, True)
                    last.then_inc(chunk_done if d % 4 == 3 else e_ready, 1)
                pe.wait_ge(o_summed, after(l * KD + (KD - 1)))
                pe.matmul(bank(6), ones[:], o_acc[:], start=True, stop=True).then_inc(o_total, 1)

                value = pe.to_reg(after(l * KD + (KD - 1)))
                pe.wait_ge(const_loaded, 16)
                pe.wait_ge(hx_made, value)
                with pe.Fori(0, 2) as i:
                    for u in range(4):
                        pe.wait_ge(gate_scaled, after(l * KD + i * 4 + (u - 2)))
                        project(l, i, J_GATE + u, u % 2)

        @block.scalar
        def _(act):
            for s in given["act"]:
                act.sem_inc(s, CREDIT)

            def hi(l, quads, j):
                s = j % RING
                act.wait_ge(raw_loaded[s], (l * SLOT_USES[s] + quads + (j // RING + 1)) * 16)
                act.activation(w_hi_t[s][:], w_raw_t[s][:], ACT.Copy).then_inc(w_hi_made, 1)

            act.wait_ge(rope_args, after(0))
            act.activation(sin_t[:], ang[:], ACT.Sin)
            act.activation(cos_t[:], turns[:], ACT.Sin).then_inc(rope_sines, 1)
            act.wait_ge(x_loaded, 16)

            with act.Fori(0, DEPTH) as l:
                act.wait_ge(x_made, after(l * KD - 1))
                for k in range(KD):
                    act.wait_ge(n_sq_used, after(l * KD + (k - 2)))
                    act.activation(n_sq[:, k % 2, :], tile(x, k), ACT.Square).then_inc(n_squared, 1)
                    if k % 2:
                        hi(l, 0, k // 2)
                act.wait_ge(n_total, after(l))
                act.activation(n_r[:], bank(7), ACT.Sqrt, bias=eps[:], scale=1.0 / D_MODEL).then_inc(n_root, 1)
                for k in range(KD):
                    act.wait_ge(n_scaled, after(l * KD + k))
                    act.activation(tile(h_hi, k), n_t[:, k % 2, :], ACT.Copy).then_inc(n_hi_made, 1)

                act.wait_ge(chunk_done, after(nth(l, 0, J_LAT)))
                act.activation(sq_a[:], bank(0), ACT.Square).then_inc(lat_squared, 1)
                act.wait_ge(chunk_done, after(nth(l, 0, J_LAT + 1)))
                act.activation(sq_b[:], bank(1), ACT.Square).then_inc(lat_squared, 1)
                hi(l, 0, J_AV)
                hi(l, 0, J_AV + 1)
                act.wait_ge(chunk_done, after(nth(l, 0, J_LAT + 2)))
                act.activation(tmp1[:], bank(2), ACT.Square).then_inc(lat_squared, 1)
                hi(l, 0, J_AV + 2)
                act.wait_ge(chunk_done, after(nth(l, 0, J_LAT + 3)))
                act.activation(sq_kr[:], bank(3), ACT.Square).then_inc(lat_squared, 1)
                hi(l, 0, J_AV + 3)
                for g in range(G):
                    act.wait_ge(chunk_done, after(nth(l, 0, J_AV + g)))
                    act.activation(tile(av_t, g), bank(6 + g % 2), ACT.Copy).then_inc(av_taken, 1)
                    if g == 0:
                        act.wait_ge(lat_total, after(l * 2))
                        act.activation(sq_b[:], bank(4), ACT.Sqrt, bias=eps[:], scale=1.0 / (2 * P)).then_inc(
                            lat_root, 1)
                        act.wait_ge(lat_total, after(l * 2 + 1))
                        act.activation(r_k[:], bank(5), ACT.Sqrt, bias=eps[:], scale=1.0 / P).then_inc(lat_root, 1)
                    if g < G - 1:
                        hi(l, 0, J_H1 + g)

                with act.Fori(0, G) as g:
                    n = l * G + g
                    act.wait_ge(chunk_done, after(nth(l, g, J_H1)))
                    hi(l, g, J_H1 + 3)
                    for b, o in ((4, sq_a), (5, sq_b), (6, sq_k)):
                        act.wait_ge(c_ready, after(n * 4 + (b - 4)))
                        act.activation(o[:], bank(b), ACT.Square).then_inc(c_squared, 1)
                    act.wait_ge(c_ready, after(n * 4 + 3))
                    act.activation(cv_hi[:], bank(7), ACT.Copy).then_inc(cv_hi_made, 1)
                    act.wait_ge(chunk_done, after(nth(l, g, J_H1 + 1)))
                    hi(l, g, J_H1 + 4)
                    act.wait_ge(chunk_done, after(nth(l, g, J_H1 + 2)))
                    act.activation(sz_c[:], bank(0), ACT.Tanh, scale=0.5).then_inc(cz_tanh, 1)
                    act.wait_ge(stat_ready, after(n * 2))
                    act.activation(small[:, 0:4], ps[:, 3 * 512:3 * 512 + 4], ACT.Sqrt, bias=eps[:],
                                   scale=1.0 / QK).then_inc(c_root, 1)
                    act.wait_ge(stat_ready, after(n * 2 + 1))
                    act.activation(r_k[:], bank(2), ACT.Sqrt, bias=eps[:], scale=1.0 / QK).then_inc(c_root, 1)
                    hi(l, g, J_H1 + 5)
                    act.wait_ge(chunk_done, after(nth(l, g, J_H1 + 3)))
                    act.activation(sz_b[:], bank(1), ACT.Tanh, scale=0.5).then_inc(bz_tanh, 1)
                    act.wait_ge(s_max, after(n))
                    for b in range(TB):
                        s = slice(ROW_AT[b], ROW_AT[b] + (b + 1) * P)
                        last = act.activation(prob[:, s], ps[:, SC + s.start:SC + s.stop], ACT.Exp,
                                              bias=small[:, 20 + b:21 + b], scale=small[:, 8 + b:9 + b],
                                              accum_out=small[:, 24 + b:25 + b])
                    last.then_inc(exp_made, 1)
                    hi(l, g, J_H1 + 6)
                    act.wait_ge(pt_ready, after(n))
                    for i, w in ((0, 512), (512, 512), (1024, 256)):
                        last = act.activation(pt_hi[:, i:i + w], ps[:, PTB + i:PTB + i + w], ACT.Copy)
                    last.then_inc(pt_hi_made, 1)

                act.wait_ge(act1_made, after(l * G + (G - 1)))
                act.dma_start(rows[:], rows_in[l].partition_broadcast(P)).then_inc(rows_loaded, 16)
                for t in range(TB):
                    act.wait_ge(ln_var, after(l * TB + t))
                    act.activation(small[:, 8:9], small[:, 7:8], ACT.Sqrt, bias=eps[:]).then_inc(ln_root, 1)

                def merge(half, j_at):
                    with act.Fori(0, 2) as i:
                        for u in range(4):
                            q = l * (2 * KD) + i * 4 + (half * KD + u)
                            act.wait_ge(m_done, after(q - 2))
                            for branch in range(2):
                                act.wait_ge(chunk_done, after(nth(l, i * 3, j_at + 3 * u + branch)))
                                act.activation(th[:, 2 * (u % 2) + branch, :], bank(4 * (1 - u % 2) + branch), ACT.Tanh,
                                               scale=0.5).then_inc(g_tanh, 1)
                                hi(l, i * 3, j_at + 3 * u + branch + 3)
                            act.wait_ge(chunk_done, after(nth(l, i * 3, j_at + 3 * u + 2)))
                            hi(l, i * 3, j_at + 3 * u + 5)

                merge(0, J_M1)

                act.wait_ge(chunk_done, after(nth(l, 0, J_MIX)))
                hi(l, 0, J_MIX + 3)

                with act.Fori(0, 2) as i:
                    for u in range(2):
                        n = l * G + i * 2 + u
                        j = J_H2 + 6 * u
                        step = Steps(act_steps, n * 6, 6)
                        act.wait_ge(act2_made, after(n - 1))
                        act.wait_ge(chunk_done, after(nth(l, i * 3, j)))
                        hi(l, i * 3, j + 3)
                        act.wait_ge(chunk_done, after(nth(l, i * 3, j + 1)))
                        act.activation(dk_hi[:], bank(1), ACT.Copy).then_inc(dk_hi_made, 1)
                        hi(l, i * 3, j + 4)
                        act.wait_ge(chunk_done, after(nth(l, i * 3, j + 2)))
                        act.activation(dv_t[:], bank(0), ACT.Copy).then_inc(dv_taken, 1)
                        hi(l, i * 3, j + 5)
                        act.wait_ge(z_ready, after(n))
                        pieces = ((0, 512), (512, 1024), (1024, TRI))
                        magnitudes, exps = [], []
                        for a, b in pieces:
                            act.activation(z_s[:, a:b], ps[:, SC + a:SC + b], ACT.Abs).then_inc(step.done, 1)
                            magnitudes.append(step.next())
                        for (a, b), k in zip(pieces, magnitudes):
                            act.wait_ge(step.done, k)
                            act.activation(z_s[:, a:b], z_s[:, a:b], ACT.Exp, scale=-1.0).then_inc(step.done, 1)
                            exps.append(step.next())
                        for (a, b), k in zip(pieces, exps):
                            act.wait_ge(step.done, k)
                            act.activation(z_s[:, a:b], z_s[:, a:b], ACT.Ln, bias=1.0).then_inc(z_log, 1)
                        act.wait_ge(chunk_done, after(nth(l, i * 3, j + 3)))
                        act.activation(a_u[:], bank(1), ACT.Copy).then_inc(au_taken, 1)
                        hi(l, i * 3, j + 6)
                        act.wait_ge(dvt_ready, after(n))
                        act.activation(dv_hi[:], bank(5), ACT.Copy).then_inc(dv_hi_made, 1)
                        act.wait_ge(cum_ready, after(n))
                        for a, b in pieces:
                            act.activation(sp[:, a:b], ps[:, SC + a:SC + b], ACT.Exp).then_inc(a_made, 1)
                        act.wait_ge(chunk_done, after(nth(l, i * 3, j + 4)))
                        act.activation(sz_a[:], bank(0), ACT.Tanh, scale=0.5).then_inc(az_tanh, 1)
                        hi(l, i * 3, j + 7)
                        act.wait_ge(chunk_done, after(nth(l, i * 3, j + 5)))
                        act.activation(sz_d[:], bank(1), ACT.Tanh, scale=0.5).then_inc(dz_tanh, 1)
                        hi(l, i * 3, j + 8)
                        step.close()

                act.wait_ge(act2_made, after(l * G + (G - 1)))
                act.dma_start(p_raw[:], p_in[l]).then_inc(p_loaded, 16)
                merge(1, J_M2)

                with act.Fori(0, 2) as i:
                    for u in range(4):
                        n = l * KD + i * 4 + u
                        act.wait_ge(chunk_done, after(nth(l, i, J_WO + u)))
                        hi(l, i, J_WO + u + 3)
                        act.wait_ge(x_moved, after(n))
                        act.wait_ge(o_summed, after(n - 2))
                        act.activation(o_sq[:, u % 2, :], tile(x, i * 4 + u), ACT.Square).then_inc(o_squared, 1)
                for d in range(KD):
                    if d % 4 == 3:
                        act.wait_ge(chunk_done, after(nth(l, 0, J_PLE + d // 4)))
                    else:
                        act.wait_ge(e_ready, after(l * (KD - 2) + (d - d // 4)))
                    act.activation(tile(e, d), bank(2 + d % 2), ACT.Copy).then_inc(e_taken, 1)
                    if d % 4 == 3:
                        hi(l, 0, J_PLE + d // 4 + 3)
                act.wait_ge(o_total, after(l))
                act.activation(o_r[:], bank(6), ACT.Sqrt, bias=eps[:], scale=1.0 / D_MODEL).then_inc(o_root, 1)
                for d in range(KD):
                    act.wait_ge(gate_scaled, after(l * KD + d))
                    if J_GATE + d + 3 < CHUNKS:
                        hi(l, 0, J_GATE + d + 3)
                    act.activation(o_t[:, d % 2, :], o_t[:, d % 2, :], ACT.Tanh, scale=0.5).then_inc(gate_tanh, 1)

        @block.vector
        def _(dve):
            for s in given["dve"]:
                dve.sem_inc(s, CREDIT)

            def low(o, src, hi_part):
                return dve.tensor_tensor(o, src, hi_part.bitcast(F32), ALU.subtract)

            def split(step, o_hi, o_lo, src):
                dve.tensor_copy(o_hi, src).then_inc(step.done, 1)
                dve.wait_ge(step.done, step.next())
                return low(o_lo, src, o_hi)

            def col(name, i=0):
                return par[:, PC[name].start + i:PC[name].start + i + 1]

            def rotate(step, o, t, scratch):
                half = ROPE // 2
                dve.tensor_tensor(o, t, cos_t[:], ALU.mult).then_inc(step.done, 1)
                dve.wait_ge(step.done, step.next())
                dve.tensor_tensor(scratch[0:half, :], t[half:ROPE, :], sin_t[half:ROPE, :], ALU.mult).then_inc(
                    step.done, 1)
                dve.wait_ge(step.done, step.next())
                dve.tensor_tensor(scratch[half:ROPE, :], t[0:half, :], sin_t[0:half, :], ALU.mult).then_inc(
                    step.done, 1)
                dve.wait_ge(step.done, step.next())
                dve.tensor_tensor(o[0:ROPE, :], o[0:ROPE, :], scratch[0:ROPE, :], ALU.add).then_inc(step.done, 1)
                dve.wait_ge(step.done, step.next())

            def steps(phase, n):
                return Steps(own[phase], n * STEPS[phase], STEPS[phase])

            step = steps("start", 0)
            dve.memset(eps[:], EPS)
            dve.wait_ge(const_loaded, 16)
            for t, name in ((ident, "ident"), (ones, "ones"), (negtri, "negtri"), (neg_i, "neg_i"), (mask_c, "mask_c"),
                            (inv_edge, "inv_edge"), (inv_win, "inv_win")):
                dve.tensor_copy(t[:], c_st[:, CC[name]])
            dve.tensor_scalar(negones[:], c_st[:, CC["ones"]], -1.0, None, ALU.mult)
            dve.tensor_copy(mask_d[:], c_st[:, CC["mask_d"]]).then_inc(consts_made, 1)
            dve.wait_ge(pos_loaded, 16)
            dve.tensor_copy(turns[:], pos_i[:]).then_inc(step.done, 1)
            dve.wait_ge(step.done, step.next())
            dve.tensor_scalar(ang[:], turns[:], c_st[:, CC["freq"]], None, ALU.mult).then_inc(step.done, 1)
            dve.wait_ge(step.done, step.next())
            dve.tensor_scalar(turns[:], ang[:], float(1 / (2 * np.pi)), None, ALU.mult).then_inc(step.done, 1)
            dve.wait_ge(step.done, step.next())
            dve.tensor_scalar(turns[:], turns[:], ROUND, None, ALU.add).then_inc(step.done, 1)
            dve.wait_ge(step.done, step.next())
            dve.tensor_scalar(turns[:], turns[:], ROUND, None, ALU.subtract).then_inc(step.done, 1)
            dve.wait_ge(step.done, step.next())
            for part in TWO_PI:
                dve.scalar_tensor_tensor(ang[:], turns[:], -part, ang[:], ALU.mult, ALU.add).then_inc(step.done, 1)
                dve.wait_ge(step.done, step.next())
            dve.tensor_scalar(ang[:], ang[:], PI_IN, -PI_IN, ALU.min, ALU.max).then_inc(step.done, 1)
            dve.wait_ge(step.done, step.next())
            dve.tensor_scalar(turns[:], ang[:], -1.0, None, ALU.mult).then_inc(step.done, 1)
            dve.wait_ge(step.done, step.next())
            dve.tensor_tensor(turns[:], turns[:], ang[:], ALU.max).then_inc(step.done, 1)
            dve.wait_ge(step.done, step.next())
            dve.tensor_scalar(turns[:], turns[:], -1.0, float(np.pi / 2), ALU.mult, ALU.add).then_inc(rope_args, 1)
            dve.wait_ge(rope_sines, after(0))
            dve.tensor_scalar(sin_t[ROPE // 2:ROPE, :], sin_t[ROPE // 2:ROPE, :], -1.0, None, ALU.mult).then_inc(
                step.done, 1)
            dve.wait_ge(step.done, step.next())
            step.close()
            dve.wait_ge(par_loaded, 16)

            with dve.Fori(0, DEPTH) as l:
                step = steps("norm", l)
                dve.wait_ge(x_made, after(l * KD - 1))
                dve.tensor_copy(par[:], par_all[:, bass.ds(l * PARAMS, PARAMS)]).then_inc(step.done, 1)
                dve.wait_ge(step.done, step.next())
                for k in range(KD):
                    dve.wait_ge(n_squared, after(l * KD + k))
                    if k:
                        dve.wait_ge(n_sq_used, after(l * KD + (k - 1)))
                        last = dve.tensor_tensor(n_acc[:], n_acc[:], n_sq[:, k % 2, :], ALU.add)
                    else:
                        last = dve.tensor_copy(n_acc[:], n_sq[:, 0, :])
                    last.then_inc(n_sq_used, 1)
                    dve.wait_ge(n_sq_used, after(l * KD + k))
                dve.wait_ge(n_root, after(l))
                dve.reciprocal(n_r[:], n_r[:]).then_inc(step.done, 1)
                dve.wait_ge(step.done, step.next())
                step.close()
                for k in range(KD + 1):
                    if k < KD:
                        dve.scalar_tensor_tensor(n_t[:, k % 2, :], tile(x, k), col("norm", k), n_r[:], ALU.mult,
                                                 ALU.mult).then_inc(n_scaled, 1)
                        dve.wait_ge(n_scaled, after(l * KD + k))
                    if k:
                        dve.wait_ge(n_hi_made, after(l * KD + (k - 1)))
                        low(tile(h_lo, k - 1), n_t[:, (k - 1) % 2, :], tile(h_hi, k - 1)).then_inc(h_made, 1)
                        dve.wait_ge(h_made, after(l * KD + (k - 1)))

                step = steps("latents", l)
                dve.memset(cs_pad[:, 0:PAD], 0.0).then_inc(step.done, 1)
                dve.wait_ge(step.done, step.next())
                dve.wait_ge(lat_squared, after(l * 4 + 1))
                dve.tensor_tensor(sq_a[:], sq_a[:], sq_b[:], ALU.add).then_inc(lat_summed, 1)
                dve.wait_ge(lat_summed, after(l))
                dve.wait_ge(lat_squared, after(l * 4 + 3))
                dve.tensor_scalar(tmp0[:], bank(3), col("kr"), None, ALU.mult).then_inc(step.done, 1)
                dve.wait_ge(step.done, step.next())
                rotate(step, krr[:], tmp0[:], prob[:, 0:SEQ])
                dve.wait_ge(lat_root, after(l * 2))
                dve.reciprocal(sq_b[:], sq_b[:]).then_inc(step.done, 1)
                dve.wait_ge(step.done, step.next())
                for k in range(2):
                    dve.scalar_tensor_tensor(tmp0[:], bank(k), col("cq", k), sq_b[:], ALU.mult, ALU.mult).then_inc(
                        step.done, 1)
                    dve.wait_ge(step.done, step.next())
                    split(step, cqn_hi[:, k, :], cqn_lo[:, k, :], tmp0[:]).then_inc(step.done, 1)
                    dve.wait_ge(step.done, step.next())
                dve.wait_ge(lat_root, after(l * 2 + 1))
                dve.reciprocal(r_k[:], r_k[:]).then_inc(step.done, 1)
                dve.wait_ge(step.done, step.next())
                dve.scalar_tensor_tensor(tmp0[:], bank(2), col("ckv"), r_k[:], ALU.mult, ALU.mult).then_inc(
                    step.done, 1)
                dve.wait_ge(step.done, step.next())
                split(step, ckvn_hi[:], ckvn_lo[:], tmp0[:]).then_inc(lat_made, 1)
                value = dve.to_reg(after(l))
                dve.wait_ge(const_loaded, 16)
                dve.wait_ge(lat_made, value)
                step.close()

                with dve.Fori(0, G) as g:
                    n = l * G + g
                    step = steps("half1", n)
                    back = PAD - (2 << g)
                    dve.compute_val(back)
                    dve.wait_ge(chunk_done, after(nth(l, g, J_H1)))
                    dve.tensor_copy(bx[:], bank(0)).then_inc(bx_taken, 1)
                    dve.wait_ge(bx_taken, after(n))
                    dve.tensor_tensor_scan(cs_pad[:, PAD:], ones[:, 0:1].to_broadcast([P, SEQ]), bx[:], 0.0,
                                           ALU.mult, ALU.add).then_inc(step.done, 1)
                    dve.wait_ge(step.done, step.next())
                    dve.tensor_tensor(diff[:], cs_pad[:, PAD:], cs_pad[:, bass.ds(back, SEQ)],
                                      ALU.subtract).then_inc(step.done, 1)
                    dve.wait_ge(step.done, step.next())
                    dve.tensor_tensor(edge[:], diff[:, 0:PAD], tile(inv_edge, g, PAD), ALU.mult).then_inc(step.done, 1)
                    dve.wait_ge(step.done, step.next())
                    dve.scalar_tensor_tensor(diff[:], diff[:], tile(inv_win, g, 1), bx[:], ALU.mult,
                                             ALU.subtract).then_inc(step.done, 1)
                    dve.wait_ge(step.done, step.next())
                    dve.tensor_tensor(diff[:, 0:PAD], edge[:], bx[:, 0:PAD], ALU.subtract).then_inc(step.done, 1)
                    dve.wait_ge(step.done, step.next())
                    split(step, pool_hi[:], pool_lo[:], diff[:]).then_inc(pooled, 1)
                    dve.wait_ge(pooled, after(n))
                    dve.wait_ge(c_squared, after(n * 3))
                    dve.tensor_scalar(qn_hi[:], bank(4), col("qn"), None, ALU.mult).then_inc(step.done, 1)
                    dve.wait_ge(step.done, step.next())
                    dve.scalar_tensor_tensor(qn_lo[:], bank(4), col("qn"), qn_hi[:].bitcast(F32), ALU.mult,
                                             ALU.subtract).then_inc(step.done, 1)
                    dve.wait_ge(step.done, step.next())
                    dve.wait_ge(c_squared, after(n * 3 + 1))
                    dve.tensor_scalar(tmp0[:], bank(5), col("qr"), None, ALU.mult).then_inc(step.done, 1)
                    dve.wait_ge(step.done, step.next())
                    rotate(step, tmp1[:], tmp0[:], r_k[:])
                    split(step, qr_hi[:], qr_lo[:], tmp1[:]).then_inc(q_made, 1)
                    dve.wait_ge(q_made, after(n))
                    dve.wait_ge(c_squared, after(n * 3 + 2))
                    dve.tensor_tensor(sq_k[:], sq_k[:], sq_kr[:], ALU.add).then_inc(sqk_made, 1)
                    dve.wait_ge(sqk_made, after(n))
                    dve.wait_ge(cv_hi_made, after(n))
                    low(cv_lo[:], bank(7), cv_hi[:]).then_inc(cv_made, 1)
                    dve.wait_ge(cv_made, after(n))
                    dve.wait_ge(chunk_done, after(nth(l, g, J_H1 + 1)))
                    dve.tensor_scalar(diff[:], bank(1), par[:, bass.ds(g + PC["pool"].start, 1)], None,
                                      ALU.mult).then_inc(pool_taken, 1)
                    dve.wait_ge(pool_taken, after(n))
                    dve.wait_ge(cz_tanh, after(n))
                    dve.scalar_tensor_tensor(sz_c[:], sz_c[:], 1.0, bank(0), ALU.add, ALU.mult).then_inc(cz_taken, 1)
                    dve.wait_ge(cz_taken, after(n))
                    dve.wait_ge(c_root, after(n * 2))
                    dve.reciprocal(small[:, 4:8], small[:, 0:4]).then_inc(step.done, 1)
                    dve.wait_ge(step.done, step.next())
                    dve.tensor_scalar(small[:, 8:12], small[:, 4:8], Q_SCALE_C, None, ALU.mult).then_inc(step.done, 1)
                    dve.wait_ge(step.done, step.next())
                    dve.tensor_scalar(small[:, 12:16], small[:, 4:8], -Q_SCALE_C, None, ALU.mult).then_inc(step.done, 1)
                    dve.wait_ge(step.done, step.next())
                    dve.wait_ge(c_root, after(n * 2 + 1))
                    dve.reciprocal(r_k[:], r_k[:]).then_inc(step.done, 1)
                    dve.wait_ge(step.done, step.next())
                    dve.scalar_tensor_tensor(tmp0[:], bank(6), col("kn"), r_k[:], ALU.mult, ALU.mult).then_inc(
                        step.done, 1)
                    dve.wait_ge(step.done, step.next())
                    dve.tensor_tensor(tmp1[:], krr[:], r_k[:], ALU.mult).then_inc(step.done, 1)
                    dve.wait_ge(step.done, step.next())
                    dve.tensor_copy(kn_hi[:], tmp0[:]).then_inc(step.done, 1)
                    dve.wait_ge(step.done, step.next())
                    dve.tensor_copy(kr_hi[:], tmp1[:]).then_inc(step.done, 1)
                    dve.wait_ge(step.done, step.next())
                    low(kn_lo[:], tmp0[:], kn_hi[:]).then_inc(step.done, 1)
                    dve.wait_ge(step.done, step.next())
                    low(kr_lo[:], tmp1[:], kr_hi[:]).then_inc(k_made, 1)
                    dve.wait_ge(k_made, after(n))
                    dve.wait_ge(bz_tanh, after(n))
                    dve.scalar_tensor_tensor(sz_b[:], sz_b[:], 1.0, bank(1), ALU.add, ALU.mult).then_inc(bz_taken, 1)
                    dve.wait_ge(bz_taken, after(n))
                    dve.wait_ge(s_ready, after(n))
                    for b in range(TB):
                        s = SC + ROW_AT[b]
                        dve.tensor_reduce(small[:, 16 + b:17 + b], ps[:, s:s + (b + 1) * P], mybir.AxisListType.X,
                                          ALU.max).then_inc(step.done, 1)
                        last = step.next()
                    dve.wait_ge(step.done, last)
                    dve.tensor_tensor(small[:, 20:24], small[:, 16:20], small[:, 12:16], ALU.mult).then_inc(s_max, 1)
                    dve.wait_ge(s_max, after(n))
                    dve.scalar_tensor_tensor(tmp0[:], diff[:], 0.5, sz_b[:], ALU.mult, ALU.mult).then_inc(step.done, 1)
                    dve.wait_ge(step.done, step.next())
                    split(step, tile(act_hi, g), tile(act_lo, g), tmp0[:]).then_inc(step.done, 1)
                    dve.wait_ge(step.done, step.next())
                    dve.wait_ge(exp_made, after(n))
                    dve.reciprocal(small[:, 28:32], small[:, 24:28]).then_inc(step.done, 1)
                    dve.wait_ge(step.done, step.next())
                    for b in range(TB):
                        s = slice(ROW_AT[b], ROW_AT[b] + (b + 1) * P)
                        last = dve.tensor_scalar(prob[:, s], prob[:, s], small[:, 28 + b:29 + b], None, ALU.mult)
                    last.then_inc(p_made, 1)
                    dve.wait_ge(p_made, after(n))
                    dve.wait_ge(pt_hi_made, after(n))
                    for i, w in ((0, 512), (512, 512), (1024, 256)):
                        last = low(pt_lo[:, i:i + w], ps[:, PTB + i:PTB + i + w], pt_hi[:, i:i + w])
                    last.then_inc(pt_made, 1)
                    dve.wait_ge(pt_made, after(n))
                    dve.wait_ge(oc_ready, after(n))
                    dve.scalar_tensor_tensor(tmp0[:], bank(2), 0.5, sz_c[:], ALU.mult, ALU.mult).then_inc(step.done, 1)
                    dve.wait_ge(step.done, step.next())
                    split(step, tile(act_hi, g + G), tile(act_lo, g + G), tmp0[:]).then_inc(act1_made, 1)
                    dve.wait_ge(act1_made, after(n))
                    step.close()

                step = steps("ln", l)
                dve.wait_ge(rows_loaded, (l + 1) * 16)
                for t in range(TB):
                    dve.wait_ge(ln_ready, after(l * TB + t))
                    dve.bn_stats(small[:, 0:6], bank(t)).then_inc(step.done, 1)
                    value = dve.to_reg(step.next())
                    dve.wait_ge(const_loaded, 16)
                    dve.wait_ge(step.done, value)
                    dve.bn_aggr(small[:, 6:8], small[:, 0:6]).then_inc(ln_var, 1)
                    dve.wait_ge(ln_var, after(l * TB + t))
                    dve.wait_ge(ln_root, after(l * TB + t))
                    dve.reciprocal(small[:, 9:10], small[:, 8:9]).then_inc(step.done, 1)
                    dve.wait_ge(step.done, step.next())
                    dve.tensor_scalar(xh[:], bank(t), small[:, 6:7], small[:, 9:10], ALU.subtract, ALU.mult).then_inc(
                        step.done, 1)
                    dve.wait_ge(step.done, step.next())
                    dve.tensor_tensor(xh[:], xh[:], rows[:, 0, :], ALU.mult).then_inc(step.done, 1)
                    dve.wait_ge(step.done, step.next())
                    dve.tensor_tensor(xh[:], xh[:], rows[:, 1, :], ALU.add).then_inc(step.done, 1)
                    dve.wait_ge(step.done, step.next())
                    last = split(step, tile(vn_hi, t), tile(vn_lo, t), xh[:])
                    if t < TB - 1:
                        last.then_inc(step.done, 1)
                        dve.wait_ge(step.done, step.next())
                last.then_inc(ln_made, 1)
                value = dve.to_reg(after(l))
                dve.wait_ge(const_loaded, 16)
                dve.wait_ge(ln_made, value)
                step.close()

                def merge(half, j_at):
                    with dve.Fori(0, 2) as i:
                        phase = f"merge{half}"
                        step = Steps(own[phase], l * 2 * STEPS[phase] + i * STEPS[phase], STEPS[phase])
                        for u in range(4):
                            q = l * (2 * KD) + i * 4 + (half * KD + u)
                            d = i * 4 + u
                            b = 4 * (1 - u % 2) + 2
                            dve.wait_ge(g_tanh, after(q * 2 + 1))
                            dve.wait_ge(y_ready, after(q))
                            dve.scalar_tensor_tensor(m_part[:, 0, :], th[:, 2 * (u % 2), :], 1.0, bank(b), ALU.add,
                                                       ALU.mult).then_inc(step.done, 1)
                            dve.wait_ge(step.done, step.next())
                            dve.wait_ge(chunk_done, after(nth(l, i * 3, j_at + 3 * u + 2)))
                            dve.scalar_tensor_tensor(m_part[:, 1, :], th[:, 2 * (u % 2) + 1, :], 1.0, bank(b + 1),
                                                     ALU.add, ALU.mult).then_inc(step.done, 1)
                            dve.wait_ge(step.done, step.next())
                            if half == 0:
                                dve.tensor_tensor(tile(merged, d), m_part[:, 0, :], m_part[:, 1, :],
                                                  ALU.add).then_inc(m_done, 1)
                                dve.wait_ge(m_done, after(q))
                            else:
                                dve.tensor_tensor(m_part[:, 0, :], m_part[:, 0, :], m_part[:, 1, :], ALU.add).then_inc(
                                    step.done, 1)
                                dve.wait_ge(step.done, step.next())
                                dve.tensor_tensor(m_part[:, 0, :], m_part[:, 0, :], tile(merged, d), ALU.add).then_inc(
                                    step.done, 1)
                                dve.wait_ge(step.done, step.next())
                                dve.tensor_scalar(tile(m_hi, d), m_part[:, 0, :], 0.5, None, ALU.mult).then_inc(
                                    step.done, 1)
                                dve.wait_ge(step.done, step.next())
                                dve.scalar_tensor_tensor(tile(m_lo, d), m_part[:, 0, :], 0.5,
                                                         tile(m_hi, d).bitcast(F32), ALU.mult,
                                                         ALU.subtract).then_inc(m_done, 1)
                                dve.wait_ge(m_done, after(q))
                        step.close()

                merge(0, J_M1)

                dve.wait_ge(w_lo_made, after(l * CHUNKS + J_MIX))
                for t in (w_hi_t[J_MIX % RING], w_lo_t[J_MIX % RING]):
                    last = dve.memset(t[P // 2:P, 0:G, 0:P // 2].bitcast(F32), 0.0)
                last.then_inc(wt_masked, 1)
                dve.wait_ge(wt_masked, after(l))
                for g in range(G):
                    if g < G - 1:
                        dve.wait_ge(mix_ready, after(l * (G - 1) + g))
                    else:
                        dve.wait_ge(chunk_done, after(nth(l, 0, J_MIX)))
                    bias = rows[:, 2, g * P:(g + 1) * P].unsqueeze(1).broadcast_to([P, TB, P])
                    dve.tensor_tensor(tile(mix_t, g).rearrange("p (t s) -> p t s", t=TB),
                                      bank(4 + g).rearrange("p (t s) -> p t s", t=TB), bias,
                                      ALU.add).then_inc(mix_taken, 1)
                    value = dve.to_reg(after(l * G + g))
                    dve.wait_ge(const_loaded, 16)
                    dve.wait_ge(mix_taken, value)

                with dve.Fori(0, 2) as i:
                    for u in range(2):
                        g = i * 2 + u
                        n = l * G + i * 2 + u
                        j = J_H2 + 6 * u
                        step = steps("half2", n)
                        dve.wait_ge(chunk_done, after(nth(l, i * 3, j)))
                        dve.tensor_scalar(dq_hi[:], bank(0), Q_SCALE_D, None, ALU.mult).then_inc(step.done, 1)
                        dve.wait_ge(step.done, step.next())
                        dve.scalar_tensor_tensor(dq_lo[:], bank(0), Q_SCALE_D, dq_hi[:].bitcast(F32), ALU.mult,
                                                 ALU.subtract).then_inc(dq_made, 1)
                        dve.wait_ge(dq_made, after(n))
                        dve.wait_ge(dk_hi_made, after(n))
                        low(dk_lo[:], bank(1), dk_hi[:]).then_inc(dk_made, 1)
                        dve.wait_ge(dk_made, after(n))
                        for k, (a, b) in enumerate(((0, 512), (512, 1024), (1024, TRI))):
                            dve.wait_ge(z_log, after(n * 3 + k))
                            dve.scalar_tensor_tensor(sp[:, a:b], ps[:, SC + a:SC + b], 0.0, z_s[:, a:b], ALU.max,
                                                     ALU.add).then_inc(step.done, 1)
                            dve.wait_ge(step.done, step.next())
                            last = split(step, s_hi[:, a:b], s_lo[:, a:b], sp[:, a:b])
                            if k < 2:
                                last.then_inc(step.done, 1)
                                dve.wait_ge(step.done, step.next())
                        last.then_inc(sp_made, 1)
                        dve.wait_ge(sp_made, after(n))
                        dve.wait_ge(dv_hi_made, after(n))
                        low(dv_lo[:], bank(5), dv_hi[:]).then_inc(dv_made, 1)
                        dve.wait_ge(dv_made, after(n))
                        for k, (a, b) in enumerate(((0, 512), (512, 1024), (1024, TRI))):
                            dve.wait_ge(a_made, after(n * 3 + k))
                            last = split(step, s_hi[:, a:b], s_lo[:, a:b], sp[:, a:b])
                            if k < 2:
                                last.then_inc(step.done, 1)
                                dve.wait_ge(step.done, step.next())
                        last.then_inc(a_split, 1)
                        dve.wait_ge(a_split, after(n))
                        dve.wait_ge(az_tanh, after(n))
                        dve.scalar_tensor_tensor(sz_a[:], sz_a[:], 1.0, bank(0), ALU.add, ALU.mult).then_inc(
                            az_taken, 1)
                        dve.wait_ge(az_taken, after(n))
                        dve.wait_ge(mix_taken, after(l * G + (G - 1)))
                        dve.tensor_tensor(tmp2[:], tile(mix_t, g), a_u[:], ALU.mult).then_inc(step.done, 1)
                        dve.wait_ge(step.done, step.next())
                        dve.scalar_tensor_tensor(tmp2[:], tmp2[:], 0.5, sz_a[:], ALU.mult, ALU.mult).then_inc(
                            step.done, 1)
                        dve.wait_ge(step.done, step.next())
                        split(step, tile(act_hi, g), tile(act_lo, g), tmp2[:]).then_inc(step.done, 1)
                        dve.wait_ge(step.done, step.next())
                        dve.wait_ge(dz_tanh, after(n))
                        dve.scalar_tensor_tensor(sz_d[:], sz_d[:], 1.0, bank(1), ALU.add, ALU.mult).then_inc(
                            dz_taken, 1)
                        dve.wait_ge(dz_taken, after(n))
                        dve.wait_ge(od_ready, after(n))
                        dve.scalar_tensor_tensor(tmp2[:], bank(6), 0.5, sz_d[:], ALU.mult, ALU.mult).then_inc(
                            step.done, 1)
                        dve.wait_ge(step.done, step.next())
                        split(step, tile(act_hi, g + G), tile(act_lo, g + G), tmp2[:]).then_inc(act2_made, 1)
                        dve.wait_ge(act2_made, after(n))
                        step.close()

                merge(1, J_M2)

                step = steps("out", l)
                dve.wait_ge(p_loaded, (l + 1) * 16)
                dve.tensor_copy(p_hi[:], p_raw[:]).then_inc(step.done, 1)
                dve.wait_ge(step.done, step.next())
                low(p_lo[:], p_raw[:], p_hi[:]).then_inc(p_split, 1)
                dve.wait_ge(p_split, after(l))
                dve.memset(o_acc[:], 0.0).then_inc(step.done, 1)
                value = dve.to_reg(step.next())
                dve.wait_ge(const_loaded, 16)
                dve.wait_ge(step.done, value)
                step.close()
                with dve.Fori(0, 2) as i:
                    for u in range(4):
                        d = i * 4 + u
                        n = l * KD + i * 4 + u
                        dve.wait_ge(chunk_done, after(nth(l, i, J_WO + u)))
                        dve.tensor_tensor(tile(x, d), tile(x, d), bank(u % 2), ALU.add).then_inc(x_moved, 1)
                        dve.wait_ge(x_moved, after(n))
                        gain = par[:, bass.ds(d + PC["ple"].start, 1)]
                        dve.tensor_scalar(tile(h_hi, d), tile(x, d), gain, None, ALU.mult).then_inc(hx_hi, 1)
                        dve.wait_ge(hx_hi, after(n))
                        dve.scalar_tensor_tensor(tile(h_lo, d), tile(x, d), gain, tile(h_hi, d).bitcast(F32), ALU.mult,
                                                 ALU.subtract).then_inc(hx_made, 1)
                        dve.wait_ge(hx_made, after(n))
                        dve.wait_ge(o_squared, after(n))
                        dve.wait_ge(o_summed, after(n - 1))
                        dve.tensor_tensor(o_acc[:], o_acc[:], o_sq[:, u % 2, :], ALU.add).then_inc(o_summed, 1)
                        dve.wait_ge(o_summed, after(n))
                dve.wait_ge(o_root, after(l))
                dve.reciprocal(o_r[:], o_r[:]).then_inc(o_inv, 1)
                value = dve.to_reg(after(l))
                dve.wait_ge(const_loaded, 16)
                dve.wait_ge(o_inv, value)

                with dve.Fori(0, 2) as i:
                    for u in range(5):
                        if u < 4:
                            dve.wait_ge(chunk_done, after(nth(l, i, J_GATE + u)))
                            dve.tensor_tensor(o_t[:, u % 2, :], bank(u % 2), o_r[:], ALU.mult).then_inc(
                                gate_scaled, 1)
                            dve.wait_ge(gate_scaled, after(l * KD + i * 4 + u))
                        if u:
                            d = i * 4 + (u - 1)
                            n = l * KD + i * 4 + (u - 1)
                            t = o_t[:, (u - 1) % 2, :]
                            dve.wait_ge(gate_tanh, after(n))
                            if u == 1:
                                dve.wait_ge(e_taken, after(l * KD + (KD - 1)))
                            dve.scalar_tensor_tensor(t, t, 1.0, tile(e, d), ALU.add, ALU.mult).then_inc(gated, 1)
                            dve.wait_ge(gated, after(n))
                            dve.scalar_tensor_tensor(tile(x, d), t, 0.5, tile(x, d), ALU.mult, ALU.add).then_inc(
                                x_made, 1)
                            dve.wait_ge(x_made, after(n))


def blocks(w):
    k, n = w.shape
    wide = -(-n // P) * P
    if wide > n:
        w = np.concatenate([w, np.zeros((k, wide - n), w.dtype)], 1)
    return w.reshape(k // P, P, wide // P, P).transpose(0, 2, 1, 3)


def weight_chunks(w, l):
    w_in = w["w_in"][l]

    def part(start, i=0, n=P):
        return list(blocks(w_in[:, start + i * P:start + i * P + n])[:, 0])

    zero = np.zeros((P, P), np.float32)
    outs = {k: blocks(w[k][l]) for k in ("w_a_out", "w_b_out", "w_c_out", "w_d_out", "w_o", "w_ple", "w_ple_gate")}
    w_uq = w["w_uq"][l].reshape(-1, G, QK)
    w_ukv = w["w_ukv"][l].reshape(P, G, 2, P)
    chunks = [part(C_Q, 0), part(C_Q, 1), part(C_KV), part(C_KR, 0, ROPE)]
    chunks += [part(A_V, g) for g in range(G)]
    for g in range(G):
        qn, qr = blocks(w_uq[:, g, :P]), blocks(w_uq[:, g, P:])
        chunks += [part(B_X, g),
                   [qn[0, 0], qn[1, 0], qr[0, 0], qr[1, 0], w_ukv[:, g, 0], w_ukv[:, g, 1], w["pool_w"][l, g], zero],
                   part(C_Z, g), part(B_Z, g)]

    def merge(a, b, names):
        for d in range(KD):
            chunks.append(part(GATES + a * D_MODEL, d))
            chunks.append(part(GATES + b * D_MODEL, d))
            chunks.append([outs[name][k, d] for name in names for k in range(G)])

    merge(1, 2, ("w_b_out", "w_c_out"))
    chunks.append([w["sgu_w"][l, g].T for g in range(G)] + [zero] * (8 - G))
    for g in range(G):
        chunks += [part(s, g) for s in (D_Q, D_K, D_V, A_U, A_Z, D_Z)]
    merge(0, 3, ("w_a_out", "w_d_out"))
    chunks += [list(outs["w_o"][:, d]) for d in range(KD)]
    chunks += [[outs["w_ple"][k, d] for d in range(4 * i, 4 * i + 4) for k in range(2)] for i in range(2)]
    chunks += [list(outs["w_ple_gate"][:, d]) for d in range(KD)]
    return np.stack([np.stack(c, 1) for c in chunks])


def constants():
    row, col = np.arange(P)[:, None], np.arange(P)[None, :]
    t = np.arange(PAD)
    win = np.array([2 << g for g in range(G)])
    half = ROPE // 2
    freq = (np.float32(10000.0) ** (-np.arange(half, dtype=np.float32) / np.float32(half))).astype(np.float32)
    parts = dict(
        ident=(row == col), ones=np.ones((P, P)), negtri=-1.0 * (row >= col), neg_i=NEG * (row == col),
        mask_c=(col // 64 > row // 64), mask_d=(row >= col),
        inv_edge=np.tile((1.0 / np.minimum(t[None, :] + 1, win[:, None])).reshape(1, -1), (P, 1)),
        inv_win=np.tile(1.0 / win[None, :], (P, 1)),
        freq=np.concatenate([freq, freq, np.zeros(P - ROPE, np.float32)])[:, None])
    return np.concatenate([np.asarray(parts[k], np.float32) for k in CC], 1)


def kernel(**inputs):
    import concourse.bacc as bacc
    from concourse.bass_utils import run_bass_kernel_spmd

    w = {k: np.asarray(v) for k, v in inputs.items()}

    def by_feature(v):
        n = -(-v.shape[1] // P) * P
        v = np.concatenate([v, np.zeros((DEPTH, n - v.shape[1]), v.dtype)], 1)
        return v.reshape(DEPTH, n // P, P).transpose(2, 0, 1)

    params = np.concatenate([by_feature(v) for v in (
        w["norm_g"], w["ple_norm_g"], w["pool_scale"], w["cq_norm_g"], w["ckv_norm_g"], w["q_norm_g"][:, :P],
        w["q_norm_g"][:, P:], w["k_norm_g"][:, :P], w["k_norm_g"][:, P:])], 2)
    arrays = {
        "x_in": w["x"][0].T.reshape(KD, P, SEQ).transpose(1, 0, 2).reshape(P, KD * SEQ),
        "p_in": w["p"][:, 0].transpose(0, 2, 1).reshape(DEPTH, 2, P, SEQ).transpose(0, 2, 1, 3),
        "pos_in": w["positions"][0],
        "w_in": np.concatenate([weight_chunks(w, l) for l in range(DEPTH)]),
        "par_in": params.reshape(P, DEPTH * PARAMS),
        "rows_in": np.stack([w["ln_v_g"], w["ln_v_b"], w["sgu_b"].reshape(DEPTH, -1)], 1),
        "const_in": constants(),
    }
    arrays = {k: np.ascontiguousarray(v) for k, v in arrays.items()}
    nc = bacc.Bacc("TRN2", target_bir_lowering=False, num_devices=1)
    aps = [nc.dram_tensor(k, v.shape, mybir.dt.from_np(v.dtype), kind="ExternalInput").ap() for k, v in arrays.items()]
    out = nc.dram_tensor("out_x", (P, KD * SEQ), F32, kind="ExternalOutput").ap()
    build(nc, *aps, out)
    r = run_bass_kernel_spmd(nc, [arrays], core_ids=[0])
    y = np.asarray(r.results[0]["out_x"])
    return np.ascontiguousarray(y.reshape(P, KD, SEQ).transpose(1, 0, 2).reshape(D_MODEL, SEQ).T)[None]
```

```python
from contextlib import ExitStack

import numpy as np

import concourse.bass as bass
from concourse import mybir

F32 = mybir.dt.float32
F32R = mybir.dt.float32r
BF16 = mybir.dt.bfloat16
I32 = mybir.dt.int32
ALU = mybir.AluOpType
ACT = mybir.ActivationFunctionType

P = 128
D_MODEL, SEQ, DEPTH = 1024, 512, 2
KD = D_MODEL // P
TB = SEQ // P
G = 4
PLE = 256
ROPE = 64
QK = P + ROPE
EPS = 1e-6
NEG = -1e30
Q_SCALE_C = QK ** -0.5
Q_SCALE_D = P ** -0.5
PAD = 16

A_U, A_V, A_Z, B_X, B_Z = 0, 512, 1024, 1536, 2048
C_Q, C_KV, C_KR, C_Z = 2560, 2816, 2944, 3008
D_Q, D_K, D_V, D_Z, GATES = 3520, 4032, 4544, 5056, 5568

J_LAT = 0
J_AV = 4
J_H0 = J_AV + G - 1
J_H1 = J_H0 + 4
J_CZ = J_H1 + 4 * (G - 1)
J_M1 = J_CZ + 1
J_MIX = J_M1 + 3 * KD
J_H2 = J_MIX + 1
J_M2 = J_H2 + 6 * G
J_WO = J_M2 + 3 * KD
J_PLE = J_WO + KD
J_GATE = J_PLE + 2
CHUNKS = J_GATE + KD
RING = 4
CREDIT = RING
SLOT_USES = [len(range(s, CHUNKS, RING)) for s in range(RING)]

W_QN, W_QR, W_KN, W_V, W_POOL = 0, 2, 4, 5, 6

def columns(*parts):
    made, at = {}, 0
    for name, width in parts:
        made[name] = slice(at, at + width)
        at += width
    return made, at


PC, PARAMS = columns(("norm", KD), ("ple", KD), ("pool", G), ("cq", 2), ("ckv", 1), ("qn", 1), ("qr", 1),
                     ("kn", 1), ("kr", 1))
CC, CONSTS = columns(("ident", P), ("ones", P), ("negtri", P), ("neg_i", P), ("mask_c", P), ("mask_d", P),
                     ("keep", 1), ("inv_edge", G * PAD), ("inv_win", G), ("freq", 1))

ROW_AT = {3: 0, 2: 512, 0: 896, 1: 1024}
COL_AT = {0: 0, 1: 512, 3: 896, 2: 1024}
TRI = 1280


TWO_PI = (6.28125, 0.0019350051879882812, 3.019916050561733e-07)
PI_IN = 3.1415925
ROUND = 12582912.0

STEPS = dict(start=12, norm=2, latents=15, front=20, back=13, ln=24, merge0=8, merge1=20, half2=20, out=2)


def nth(l, quads, j):
    return l * CHUNKS + quads * RING + j




def after(n):
    return n + (1 + CREDIT)


class Steps:

    def __init__(self, done, base, per):
        self.done, self.base, self.per, self.n = done, base, per, 0

    def next(self):
        self.n += 1
        return self.base + self.n

    def close(self):
        assert self.n == self.per, f"{self.n} steps, not {self.per}"


def build(nc, x_in, p_in, pos_in, w_in, par_in, rows_in, const_in, out):
    ctx = ExitStack()
    with ctx:
        def sb(name, shape, dt=F32):
            return ctx.enter_context(nc.sbuf_tensor(name, shape, dt))

        x = sb("x", [P, KD * SEQ])
        h_hi = sb("h_hi", [P, KD * SEQ], F32R)
        h_lo = sb("h_lo", [P, KD * SEQ], F32R)
        act_hi = sb("act_hi", [P, 2 * G * SEQ], F32R)
        act_lo = sb("act_lo", [P, 2 * G * SEQ], F32R)
        w_hi_t = [sb(f"w_hi{s}", [P, 8, P], F32R) for s in range(RING)]
        ident = sb("ident", [P, P])
        ones = sb("ones", [P, P])
        negtri = sb("negtri", [P, P], F32R)
        negones = sb("negones", [P, P], F32R)
        neg_i = sb("neg_i", [P, P], BF16)
        mask_c = sb("mask_c", [P, P], BF16)
        mask_d = sb("mask_d", [P, P], BF16)
        keep = sb("keep", [P, 1])
        inv_edge = sb("inv_edge", [P, G * PAD])
        inv_win = sb("inv_win", [P, G])
        cos_t = sb("cos_t", [P, SEQ])
        sin_t = sb("sin_t", [P, SEQ])
        par_all = sb("par_all", [P, DEPTH * PARAMS])
        par = sb("par", [P, PARAMS])
        small = sb("small", [P, 40])
        edge = sb("edge", [P, PAD])
        eps = sb("eps", [P, 1])

        ring_at = (nc.sbuf_base + 31) // 32 * 32
        CH = 8 * P * 4
        ARENA = 88 * 1024
        sb("arena", [P, (RING * CH + ARENA) // 4])
        arena_at = ring_at + RING * CH

        def at(name, offset, shape, dt=F32, base=arena_at):
            return nc.alloc_sbuf_tensor_at(name, shape, dt, offset=base + offset)

        w_raw_t = [at(f"w_raw{s}", s * CH, [P, 8, P], F32, ring_at) for s in range(RING)]
        w_lo_t = [at(f"w_lo{s}", s * CH, [P, 8, P], F32R, ring_at) for s in range(RING)]

        K = 1024

        def plan(start, *items):
            made, o = [], start
            for name, shape, dt in items:
                made.append(at(name, o, [P, *shape], dt))
                o += -(-int(np.prod(shape)) * 4 // 32) * 32
            assert o <= ARENA, (items, o)
            return made

        cqn_hi, cqn_lo, ckvn_hi, ckvn_lo, krr, sq_kr = plan(
            0, ("cqn_hi", [2, SEQ], F32R), ("cqn_lo", [2, SEQ], F32R), ("ckvn_hi", [SEQ], F32R),
            ("ckvn_lo", [SEQ], F32R), ("krr", [SEQ], F32), ("sq_kr", [SEQ], F32))
        (qn_hi, qn_lo, qr_hi, qr_lo, kn_hi, kn_lo, kr_hi, kr_lo, cv_hi, cv_lo, sq_a, sq_b, sq_k, tmp0, tmp1, r_k,
         prob, pt_hi, pt_lo, sz_c, bx, cs_pad, diff, qr_gained, pool_hi, pool_lo, sz_b) = plan(
            16 * K,
            *[(n, [SEQ], F32R) for n in ("qn_hi", "qn_lo", "qr_hi", "qr_lo", "kn_hi", "kn_lo", "kr_hi", "kr_lo",
                                         "cv_hi", "cv_lo")],
            *[(n, [SEQ], F32) for n in ("sq_a", "sq_b", "sq_k", "tmp0", "tmp1", "r_k")],
            ("prob", [TRI], F32), ("pt_hi", [TRI], F32R), ("pt_lo", [TRI], F32R),
            ("sz_c", [SEQ], F32), ("bx", [SEQ], F32), ("cs_pad", [SEQ + PAD], F32),
            ("diff", [SEQ], F32), ("qr_gained", [SEQ], F32), ("pool_hi", [SEQ], F32R), ("pool_lo", [SEQ], F32R),
            ("sz_b", [SEQ], F32))
        n_t, n_acc, n_r = plan(16 * K, ("n_t", [2, SEQ], F32), ("n_acc", [SEQ], F32), ("n_r", [SEQ], F32))
        (n_sq,) = plan(28 * K, ("n_sq", [KD * SEQ], F32))
        (av_t,) = plan(80 * K, ("av_t", [G * SEQ], F32))
        (mix_t,) = plan(80 * K, ("mix_t", [G * SEQ], F32))
        (merged,) = plan(0, ("merged", [KD * SEQ], F32))
        m_hi, m_lo = plan(16 * K, ("m_hi", [KD * SEQ], F32R), ("m_lo", [KD * SEQ], F32R))
        th, m_part = plan(48 * K, ("th", [4, SEQ], F32), ("m_part", [2, SEQ], F32))
        rows, xh = plan(28 * K, ("rows", [3, SEQ], F32), ("xh", [TB, SEQ], F32))
        vn_hi, vn_lo = plan(60 * K, ("vn_hi", [TB * SEQ], F32R), ("vn_lo", [TB * SEQ], F32R))
        (dq_hi, dq_lo, dk_hi, dk_lo, dv_t, dv_hi, dv_lo, z_s, sp, s_hi, s_lo, a_u, sz_a, sz_d, tmp2) = plan(
            16 * K,
            *[(n, [SEQ], F32R) for n in ("dq_hi", "dq_lo", "dk_hi", "dk_lo")], ("dv_t", [SEQ], F32),
            *[(n, [SEQ], F32R) for n in ("dv_hi", "dv_lo")],
            ("z_s", [TRI], F32), ("sp", [TRI], F32), ("s_hi", [TRI], F32R), ("s_lo", [TRI], F32R),
            *[(n, [SEQ], F32) for n in ("a_u", "sz_a", "sz_d", "tmp2")])
        p_raw, p_hi, p_lo, e = plan(60 * K, ("p_raw", [2, SEQ], F32), ("p_hi", [2, SEQ], F32R),
                                    ("p_lo", [2, SEQ], F32R), ("e", [KD * SEQ], F32))
        o_acc, o_sq, o_r, o_t = plan(48 * K, ("o_acc", [SEQ], F32), ("o_sq", [2, SEQ], F32), ("o_r", [SEQ], F32),
                                     ("o_t", [2, SEQ], F32))
        c_st, pos_i, ang, turns = plan(0, ("c_st", [CONSTS], F32), ("pos_i", [SEQ], I32), ("ang", [SEQ], F32),
                                       ("turns", [SEQ], F32))

        ps = ctx.enter_context(nc.psum_tensor("ps", [P, 8 * 512], F32))

        def bank(b, n=512):
            return ps[:, b * 512:b * 512 + n]

        SC = 2 * 512
        PTB = 5 * 512

        given = {"pe": [], "act": [], "dve": [], "pool": []}

        def sem(name):
            return ctx.enter_context(nc.semaphore(name))

        def signals(engine, names):
            made = [sem(n) for n in names.split()]
            given[engine] += made
            return made if len(made) > 1 else made[0]

        x_loaded, pos_loaded = [sem(f"x_loaded{d}") for d in range(KD)], sem("pos_loaded")
        par_loaded, const_loaded = sem("par_loaded"), sem("const_loaded")
        rows_loaded, p_loaded, out_stored = sem("rows_loaded"), sem("p_loaded"), sem("out_stored")
        raw_loaded = [sem(f"raw_loaded{s}") for s in range(RING)]
        w_hi_made = signals("act", "w_hi_made")
        w_lo_made, mix_lo_made, mix_hi_kept = signals("pool", "w_lo_made mix_lo_made mix_hi_kept")
        chunk_done = signals("pe", "chunk_done")
        consts_made, rope_args, n_scaled, h_made = signals(
            "dve", "consts_made rope_args n_scaled h_made")
        n_zeroed, n_summed, n_diag = signals("dve", "n_zeroed n_summed n_diag")
        rope_sines, n_squared, n_root, n_hi_made = signals("act", "rope_sines n_squared n_root n_hi_made")
        n_total, n_spread = signals("pe", "n_total n_spread")
        lat_total, lat_spread = signals("pe", "lat_total lat_spread")
        lat_squared, lat_root = signals("act", "lat_squared lat_root")
        av_taken = signals("act", "av_taken")
        lat_summed, kr_taken, lat_diag, lat_made = signals("dve", "lat_summed kr_taken lat_diag lat_made")
        c_ready, stat_ready, rk_ready, s_ready, cz_ready, pt_ready, oc_ready = signals(
            "pe", "c_ready stat_ready rk_ready s_ready cz_ready pt_ready oc_ready")
        bx_taken, qn_hi_made, qr_scaled, c_squared, cv_hi_made, c_root, exp_made, pt_hi_made, cz_tanh, bz_tanh = signals(
            "act", "bx_taken qn_hi_made qr_scaled c_squared cv_hi_made c_root exp_made pt_hi_made cz_tanh bz_tanh")
        (pooled, qn_taken, rk_made, q_made, sqk_made, cv_made, pool_taken, k_made, s_max, p_made, pt_made, cz_taken,
         bz_taken,
         act1_made) = signals(
            "dve", "pooled qn_taken rk_made q_made sqk_made cv_made pool_taken k_made s_max p_made pt_made cz_taken "
                   "bz_taken "
                   "act1_made")
        ln_ready, mix_ready, y_ready = signals("pe", "ln_ready mix_ready y_ready")
        ln_root, g_tanh = signals("act", "ln_root g_tanh")
        ln_var, ln_taken, ln_made, mix_taken = signals("dve", "ln_var ln_taken ln_made mix_taken")
        m_done = signals("dve", "m_done")
        z_ready, dvt_ready, cum_ready, od_ready = signals("pe", "z_ready dvt_ready cum_ready od_ready")
        dv_taken, dk_hi_made, dv_hi_made, z_log, a_made, au_taken, az_tanh, dz_tanh = signals(
            "act", "dv_taken dk_hi_made dv_hi_made z_log a_made au_taken az_tanh dz_tanh")
        dq_made, dk_made, sp_made, dv_made, a_split, az_taken, dz_taken, act2_made = signals(
            "dve", "dq_made dk_made sp_made dv_made a_split az_taken dz_taken act2_made")
        e_ready, o_total = signals("pe", "e_ready o_total")
        o_squared, o_root, gate_tanh = signals("act", "o_squared o_root gate_tanh")
        e_taken = signals("act", "e_taken")
        p_split, hx_hi, hx_made, o_inv, gated = signals("dve", "p_split hx_hi hx_made o_inv gated")
        x_moved, x_made, o_summed, gate_scaled = signals("dve", "x_moved x_made o_summed gate_scaled")
        act_steps = sem("act_steps")
        own = {k: sem(f"dve_steps_{k}") for k in STEPS}

        block = ctx.enter_context(nc.Block())

        def col(name, i=0):
            return par[:, PC[name].start + i:PC[name].start + i + 1]

        def tile(t, i, n=SEQ):
            return t[:, bass.ds(i * n, n)] if not isinstance(i, int) else t[:, i * n:(i + 1) * n]

        @block.sync
        def _(sync):
            def load(l, quads, j, before):
                s = j % RING
                sync.wait_ge(chunk_done, after(l * CHUNKS + quads * RING + (before - 1)))
                sync.dma_start(w_raw_t[s][:], w_in[l * CHUNKS + quads * RING + j]).then_inc(raw_loaded[s], 16)

            sync.dma_start(c_st[:], const_in).then_inc(const_loaded, 16)
            sync.dma_start(par_all[:], par_in).then_inc(par_loaded, 16)
            sync.dma_start(pos_i[:], pos_in.partition_broadcast(P)).then_inc(pos_loaded, 16)
            for d in range(KD):
                sync.dma_start(x[:, d * SEQ:(d + 1) * SEQ], x_in[:, d * SEQ:(d + 1) * SEQ]).then_inc(x_loaded[d], 16)
            with sync.Fori(0, DEPTH) as l:
                for j in range(RING):
                    load(l, 0, j, (CHUNKS - 1 - j) // RING * RING + j + 1 - CHUNKS)
                full = CHUNKS // RING
                with sync.Fori(1, full) as quads:
                    for j in range(RING):
                        load(l, quads, j, j + 1 - RING)
                for j in range(RING * full, CHUNKS):
                    load(l, 0, j, j + 1 - RING)
            for d in range(KD):
                sync.wait_ge(x_made, after((DEPTH - 1) * KD + d))
                sync.dma_start(out[:, d * SEQ:(d + 1) * SEQ], tile(x, d)).then_inc(out_stored, 16)
            sync.wait_ge(out_stored, 16 * KD)

        @block.gpsimd
        def _(pool):
            for s in given["pool"]:
                pool.sem_inc(s, CREDIT)

            def lo(l, quads, j):
                s = j % RING
                pool.wait_ge(w_hi_made, after(nth(l, quads, j)))
                pool.tensor_tensor(w_lo_t[s][:], w_raw_t[s][:], w_hi_t[s][:].bitcast(F32),
                                   ALU.subtract).then_inc(w_lo_made, 1)

            for d in range(1, KD):
                pool.wait_ge(n_squared, after(d))
                if d == 1:
                    pool.tensor_tensor(n_acc[:], tile(n_sq, 0), tile(n_sq, 1), ALU.add).then_inc(n_summed, 2)
                else:
                    pool.wait_ge(n_summed, after(d - 1))
                    pool.tensor_tensor(n_acc[:], n_acc[:], tile(n_sq, d), ALU.add).then_inc(n_summed, 1)

            with pool.Fori(0, DEPTH) as l:
                full = CHUNKS // RING
                assert J_MIX % RING == 0
                pool.wait_ge(consts_made, after(0))
                with pool.Fori(0, J_MIX // RING) as quads:
                    for j in range(RING):
                        lo(l, quads, j)
                s = J_MIX % RING
                pool.wait_ge(w_hi_made, after(nth(l, 0, J_MIX)))
                pool.tensor_tensor(w_lo_t[s][:], w_raw_t[s][:], w_hi_t[s][:].bitcast(F32), ALU.subtract).then_inc(
                    mix_lo_made, 1)
                pool.wait_ge(mix_lo_made, after(l))
                kept = keep[:].unsqueeze(1).broadcast_to([P, G, P // 2])
                for t in (w_hi_t[s], w_lo_t[s]):
                    part = t[:, 0:G, 0:P // 2]
                    pool.tensor_tensor(part, part.bitcast(F32), kept, ALU.mult).then_inc(
                        mix_hi_kept if t is w_hi_t[s] else w_lo_made, 1)
                pool.wait_ge(mix_hi_kept, after(l))
                pool.wait_ge(w_lo_made, after(nth(l, 0, J_MIX)))
                for j in range(1, RING):
                    lo(l, 0, J_MIX + j)
                with pool.Fori(J_MIX // RING + 1, full) as quads:
                    for j in range(RING):
                        lo(l, quads, j)
                for j in range(RING * full, CHUNKS):
                    lo(l, 0, j)

        @block.tensor
        def _(pe):
            for s in given["pe"]:
                pe.sem_inc(s, CREDIT)

            def chunk(l, quads, j):
                pe.wait_ge(w_lo_made, after(nth(l, quads, j)))
                return w_hi_t[j % RING], w_lo_t[j % RING]

            def mm3(o, a_hi, a_lo, b_hi, b_lo, first=True, last=True, skip=False):
                pe.matmul(o, a_hi, b_hi, start=first, stop=False, skip_group_check=skip)
                pe.matmul(o, a_hi, b_lo, start=False, stop=False, skip_group_check=skip)
                return pe.matmul(o, a_lo, b_hi, start=False, stop=last, skip_group_check=skip)

            def project_k(w, o, k):
                return mm3(o, w[0][:, k, :], w[1][:, k, :], tile(h_hi, k), tile(h_lo, k), k == 0, k == KD - 1)

            def project(l, quads, j, b):
                w = chunk(l, quads, j)
                for k in range(KD):
                    last = project_k(w, bank(b), k)
                last.then_inc(chunk_done, 1)

            def by_token(b, column, squares):
                for t in range(TB):
                    o = ps[:, b * 512 + column + t:b * 512 + column + t + 1]
                    last = pe.matmul(o, tile(squares, t, P), ones[:, 0:1], start=True, stop=True)
                return last

            pe.wait_ge(consts_made, after(0))
            with pe.Fori(0, DEPTH) as l:
                pe.wait_ge(n_summed, after(l * KD + (KD - 1)))
                by_token(7, 0, n_acc).then_inc(n_total, 1)
                pe.wait_ge(n_diag, after(l))
                pe.matmul(bank(6), ones[:], n_r[:], start=True, stop=True).then_inc(n_spread, 1)

                w0, w1 = chunk(l, 0, J_LAT), chunk(l, 0, J_LAT + 1)
                for k in range(KD):
                    pe.wait_ge(h_made, after(l * KD + k))
                    last0 = project_k(w0, bank(0), k)
                    last1 = project_k(w1, bank(1), k)
                last0.then_inc(chunk_done, 1)
                last1.then_inc(chunk_done, 1)
                project(l, 0, J_LAT + 2, 2)
                project(l, 0, J_LAT + 3, 3)
                for g in range(G - 1):
                    if g == 2:
                        pe.wait_ge(av_taken, after(l * G))
                    project(l, 0, J_AV + g, 6 + g % 2)
                    if g == 0:
                        pe.wait_ge(lat_summed, after(l))
                        by_token(4, 0, sq_a)
                        pe.wait_ge(lat_squared, after(l * 4 + 3))
                        by_token(4, 4, tmp1).then_inc(lat_total, 1)
                    if g == 1:
                        pe.wait_ge(lat_diag, after(l))
                        pe.matmul(bank(5), ones[:], sq_b[:], start=True, stop=True)
                        pe.matmul(bank(4), ones[:], r_k[:], start=True, stop=True).then_inc(lat_spread, 1)

                def pool_input(quads, j, n):
                    pe.wait_ge(bz_taken, after(n - 1))
                    project(l, quads, j, 0)

                def head_products(quads, j, n):
                    w_hi, w_lo = chunk(l, quads, j)
                    pe.wait_ge(act1_made, after(n - 2))
                    for b, at_ in ((5, W_QN), (6, W_QR)):
                        mm3(bank(b), w_hi[:, at_, :], w_lo[:, at_, :], cqn_hi[:, 0, :], cqn_lo[:, 0, :], True, False)
                        mm3(bank(b), w_hi[:, at_ + 1, :], w_lo[:, at_ + 1, :], cqn_hi[:, 1, :], cqn_lo[:, 1, :], False,
                            True).then_inc(c_ready, 1)
                    mm3(bank(7), w_hi[:, W_KN, :], w_lo[:, W_KN, :], ckvn_hi[:], ckvn_lo[:]).then_inc(c_ready, 1)
                    pe.wait_ge(cv_made, after(n - 1))
                    for t in range(TB):
                        last = mm3(ps[:, 512 + t * P:512 + (t + 1) * P], tile(ckvn_hi, t, P), tile(ckvn_lo, t, P),
                                   w_hi[:, W_V, :], w_lo[:, W_V, :])
                    last.then_inc(c_ready, 1)

                def norms(n):
                    pe.wait_ge(c_squared, after(n * 3 + 2))
                    pe.wait_ge(sqk_made, after(n))
                    pe.wait_ge(pt_made, after(n - 1))
                    for t in range(TB):
                        o = ps[:, 4 * 512 + t:4 * 512 + t + 1]
                        pe.matmul(o, tile(sq_a, t, P), ones[:, 0:1], start=True, stop=False)
                        pe.matmul(o, tile(sq_b, t, P), ones[:, 0:1], start=False, stop=True)
                        last = pe.matmul(ps[:, 4 * 512 + 4 + t:4 * 512 + 5 + t], tile(sq_k, t, P), ones[:, 0:1],
                                         start=True, stop=True)
                    last.then_inc(stat_ready, 1)

                def pool_product(j, n):
                    pe.wait_ge(pooled, after(n))
                    mm3(bank(2), w_hi_t[j % RING][:, W_POOL, :], w_lo_t[j % RING][:, W_POOL, :], pool_hi[:],
                        pool_lo[:]).then_inc(chunk_done, 2)

                def k_inverse(n):
                    pe.wait_ge(q_made, after(n))
                    pe.wait_ge(rk_made, after(n))
                    pe.matmul(bank(6), ones[:], r_k[:], start=True, stop=True).then_inc(rk_ready, 1)

                def scores(n):
                    pe.wait_ge(pool_taken, after(n))
                    pe.wait_ge(k_made, after(n))
                    for b in (3, 2, 0, 1):
                        o = ps[:, SC + ROW_AT[b]:SC + ROW_AT[b] + (b + 1) * P]
                        keys = (b + 1) * P
                        mm3(o, tile(qn_hi, b, P), tile(qn_lo, b, P), kn_hi[:, 0:keys], kn_lo[:, 0:keys], b != 0,
                            False, True)
                        mm3(o, tile(qr_hi, b, P), tile(qr_lo, b, P), kr_hi[:, 0:keys], kr_lo[:, 0:keys], False,
                            False, True)
                        o = ps[:, SC + ROW_AT[b] + b * P:SC + ROW_AT[b] + (b + 1) * P]
                        last = pe.matmul(o, neg_i[:], mask_c[:], start=False, stop=True, skip_group_check=True)
                        if b != 2:
                            last.then_inc(s_ready, 1)

                def to_keys(n):
                    pe.wait_ge(p_made, after(n))
                    for kb in (0, 1, 3, 2):
                        for qb in range(kb, TB):
                            o = SC + COL_AT[kb] + (qb - kb) * P
                            i = ROW_AT[qb] + kb * P
                            last = pe.transpose(ps[:, o:o + P], prob[:, i:i + P], ident[:])
                    last.then_inc(pt_ready, 1)

                def attend(n):
                    pe.wait_ge(pt_made, after(n))
                    for kb in range(TB):
                        c = slice(COL_AT[kb], COL_AT[kb] + SEQ - kb * P)
                        last = mm3(ps[:, 5 * 512 + kb * P:6 * 512], tile(cv_hi, kb, P), tile(cv_lo, kb, P),
                                   pt_hi[:, c], pt_lo[:, c], kb == 0, kb == TB - 1)
                    last.then_inc(oc_ready, 1)

                first = l * G
                pe.wait_ge(kr_taken, after(l))
                project(l, 0, J_H0, 3)
                pe.wait_ge(lat_made, after(l))
                pe.wait_ge(av_taken, after(l * G + (G - 2)))
                head_products(0, J_H0 + 1, first)
                pe.wait_ge(bx_taken, after(first))
                w = chunk(l, 0, J_H0 + 2)
                for k in range(KD):
                    if k == KD // 2:
                        norms(first)
                    project_k(w, bank(3), k)
                k_inverse(first)
                pool_product(J_H0 + 1, first)
                project(l, 0, J_H0 + 3, 0)
                value = pe.to_reg(after(l * G + (G - 1)))
                pe.wait_ge(const_loaded, 16)
                pe.wait_ge(av_taken, value)
                with pe.Fori(0, G - 1) as g:
                    n = l * G + g
                    following = l * G + 1 + g
                    scores(n)
                    pool_input(g, J_H1, following)
                    to_keys(n)
                    head_products(g, J_H1 + 1, following)
                    pe.wait_ge(bx_taken, after(following))
                    w = chunk(l, g, J_H1 + 2)
                    for k in range(KD):
                        last = project_k(w, bank(0), k)
                    last.then_inc(cz_ready, 1)
                    norms(following)
                    pe.wait_ge(qn_taken, after(following))
                    attend(n)
                    k_inverse(following)
                    pool_product(J_H1 + 1, following)
                    pe.wait_ge(cz_taken, after(n))
                    project(l, g, J_H1 + 3, 0)
                final = l * G + (G - 1)
                scores(final)
                pe.wait_ge(bz_taken, after(final))
                project(l, 0, J_CZ, 0)
                to_keys(final)

                def av_by_token(t):
                    for g in range(G):
                        last = pe.transpose(ps[:, t * 512 + g * P:t * 512 + (g + 1) * P],
                                            av_t[:, g * SEQ + t * P:g * SEQ + (t + 1) * P], ident[:])
                    last.then_inc(ln_ready, 1)

                pe.wait_ge(cz_taken, after(final))
                pe.wait_ge(cv_made, after(final))
                av_by_token(0)
                av_by_token(1)
                attend(final)
                av_by_token(2)
                av_by_token(3)

                def merge(half, j_at):
                    with pe.Fori(0, 2) as i:
                        for u in range(4):
                            q = l * (2 * KD) + i * 4 + (half * KD + u)
                            b = 4 * (1 - u % 2)
                            pe.wait_ge(m_done, after(q - 2))
                            if half == 0 and u == 1:
                                pe.wait_ge(ln_taken, after(l * TB + (TB - 1)))
                            project(l, i * 3, j_at + 3 * u, b)
                            if u == 0:
                                pe.wait_ge(act2_made if half else act1_made, after(l * G + (G - 1)))
                            project(l, i * 3, j_at + 3 * u + 1, b + 1)
                            w_hi, w_lo = chunk(l, i * 3, j_at + 3 * u + 2)
                            for branch in range(2):
                                for k in range(G):
                                    last = mm3(bank(b + 2 + branch), w_hi[:, branch * G + k, :],
                                               w_lo[:, branch * G + k, :], tile(act_hi, branch * G + k),
                                               tile(act_lo, branch * G + k), k == 0, k == G - 1)
                                last.then_inc(chunk_done if branch else y_ready, 1)

                merge(0, J_M1)

                pe.wait_ge(m_done, after(l * (2 * KD) + (KD - 2)))
                w_hi, w_lo = chunk(l, 0, J_MIX)
                pe.wait_ge(ln_made, after(l))
                for g in range(G):
                    for t in range(TB):
                        i = t * SEQ + g * P
                        o = (4 + g) * 512 + t * P
                        last = mm3(ps[:, o:o + P], vn_hi[:, i:i + P], vn_lo[:, i:i + P], w_hi[:, g, :], w_lo[:, g, :])
                    last.then_inc(mix_ready if g < G - 1 else chunk_done, 1)

                value = pe.to_reg(after(l * (2 * KD) + (KD - 1)))
                pe.wait_ge(const_loaded, 16)
                pe.wait_ge(m_done, value)
                with pe.Fori(0, 2) as i:
                    for u in range(2):
                        n = l * G + i * 2 + u
                        j = J_H2 + 6 * u
                        pe.wait_ge(az_taken, after(n - 1))
                        project(l, i * 3, j, 0)
                        pe.wait_ge(dz_taken, after(n - 1))
                        project(l, i * 3, j + 1, 1)
                        pe.wait_ge(dq_made, after(n))
                        project(l, i * 3, j + 2, 0)
                        if u == 0:
                            pe.wait_ge(mix_taken, after(l * G + (G - 1)))
                        pe.wait_ge(dk_made, after(n))
                        for kb in (0, 1, 3, 2):
                            c = SC + COL_AT[kb]
                            mm3(ps[:, c:c + SEQ - kb * P], tile(dk_hi, kb, P), tile(dk_lo, kb, P),
                                dq_hi[:, kb * P:SEQ], dq_lo[:, kb * P:SEQ], kb != 3, False, True)
                            last = pe.matmul(ps[:, c:c + P], neg_i[:], mask_d[:], start=False, stop=False,
                                             skip_group_check=True)
                        last.then_inc(z_ready, 1)
                        project(l, i * 3, j + 3, 1)
                        pe.wait_ge(dv_taken, after(n))
                        for t in range(TB):
                            last = pe.transpose(ps[:, 5 * 512 + t * P:5 * 512 + (t + 1) * P], tile(dv_t, t, P),
                                                ident[:])
                        last.then_inc(dvt_ready, 1)
                        project(l, i * 3, j + 4, 0)
                        pe.wait_ge(sp_made, after(n))
                        for kb in range(TB):
                            for jb in range(kb, TB):
                                c = SC + COL_AT[kb] + (jb - kb) * P
                                s = slice(COL_AT[jb], COL_AT[jb] + SEQ - jb * P)
                                o = ps[:, c:c + SEQ - jb * P]
                                m = negtri if jb == kb else negones
                                pe.matmul(o, m[:], s_hi[:, s], start=False, stop=False, skip_group_check=True)
                                last = pe.matmul(o, m[:], s_lo[:, s], start=False, stop=jb == TB - 1,
                                                 skip_group_check=True)
                        last.then_inc(cum_ready, 1)
                        pe.wait_ge(au_taken, after(n))
                        project(l, i * 3, j + 5, 1)
                        pe.wait_ge(a_split, after(n))
                        pe.wait_ge(dv_made, after(n))
                        pe.wait_ge(act2_made, after(n - 1))
                        for kb in range(TB):
                            c = slice(COL_AT[kb], COL_AT[kb] + SEQ - kb * P)
                            last = mm3(ps[:, 6 * 512 + kb * P:7 * 512], tile(dv_hi, kb, P), tile(dv_lo, kb, P),
                                       s_hi[:, c], s_lo[:, c], kb == 0, kb == TB - 1)
                        last.then_inc(od_ready, 1)

                merge(1, J_M2)

                value = pe.to_reg(after(l * (2 * KD) + (2 * KD - 2)))
                pe.wait_ge(const_loaded, 16)
                pe.wait_ge(m_done, value)
                with pe.Fori(0, 2) as i:
                    for u in range(4):
                        n = l * KD + i * 4 + u
                        pe.wait_ge(x_moved, after(n - 2))
                        w_hi, w_lo = chunk(l, i, J_WO + u)
                        for k in range(KD):
                            if u == 0 and k == KD - 1:
                                pe.wait_ge(m_done, after(l * (2 * KD) + (2 * KD - 1)))
                            last = mm3(bank(4 + u % 2), w_hi[:, k, :], w_lo[:, k, :], tile(m_hi, k), tile(m_lo, k),
                                       k == 0, k == KD - 1)
                        last.then_inc(chunk_done, 1)

                pe.wait_ge(p_split, after(l))
                for d in range(KD):
                    if d % 4 == 0:
                        w_hi, w_lo = chunk(l, 0, J_PLE + d // 4)
                    pe.wait_ge(e_taken, after(l * KD + (d - 2)))
                    mm3(bank(2 + d % 2), w_hi[:, d % 4 * 2, :], w_lo[:, d % 4 * 2, :], p_hi[:, 0, :], p_lo[:, 0, :],
                        True, False)
                    last = mm3(bank(2 + d % 2), w_hi[:, d % 4 * 2 + 1, :], w_lo[:, d % 4 * 2 + 1, :], p_hi[:, 1, :],
                               p_lo[:, 1, :], False, True)
                    last.then_inc(chunk_done if d % 4 == 3 else e_ready, 1)
                pe.wait_ge(o_summed, after(l * KD + (KD - 1)))
                pe.matmul(bank(6), ones[:], o_acc[:], start=True, stop=True).then_inc(o_total, 1)

                value = pe.to_reg(after(l * KD + (KD - 1)))
                pe.wait_ge(const_loaded, 16)
                pe.wait_ge(hx_made, value)
                with pe.Fori(0, 2) as i:
                    for u in range(4):
                        pe.wait_ge(gate_scaled, after(l * KD + i * 4 + (u - 2)))
                        project(l, i, J_GATE + u, u % 2)

        @block.scalar
        def _(act):
            for s in given["act"]:
                act.sem_inc(s, CREDIT)

            def hi(l, quads, j):
                s = j % RING
                act.wait_ge(raw_loaded[s], (l * SLOT_USES[s] + quads + (j // RING + 1)) * 16)
                act.activation(w_hi_t[s][:], w_raw_t[s][:], ACT.Copy).then_inc(w_hi_made, 1)

            def square(d):
                act.activation(tile(n_sq, d), tile(x, d), ACT.Square).then_inc(n_squared, 1)

            for d in range(KD):
                act.wait_ge(x_loaded[d], 16)
                square(d)
            act.wait_ge(rope_args, after(0))
            act.activation(sin_t[:], ang[:], ACT.Sin)
            act.activation(cos_t[:], turns[:], ACT.Sin).then_inc(rope_sines, 1)

            with act.Fori(0, DEPTH) as l:
                hi(l, 0, 0)
                hi(l, 0, 1)
                act.wait_ge(n_total, after(l))
                act.activation(small[:, 0:4], ps[:, 7 * 512:7 * 512 + 4], ACT.Sqrt, bias=eps[:],
                               scale=1.0 / D_MODEL).then_inc(n_root, 1)
                for k in range(KD):
                    act.wait_ge(n_scaled, after(l * KD + k))
                    act.activation(tile(h_hi, k), n_t[:, k % 2, :], ACT.Copy).then_inc(n_hi_made, 1)
                    if k in (3, 5):
                        hi(l, 0, 2 + k // 5)

                act.wait_ge(chunk_done, after(nth(l, 0, J_LAT)))
                act.activation(sq_a[:], bank(0), ACT.Square).then_inc(lat_squared, 1)
                act.wait_ge(chunk_done, after(nth(l, 0, J_LAT + 1)))
                act.activation(sq_b[:], bank(1), ACT.Square).then_inc(lat_squared, 1)
                hi(l, 0, J_AV)
                hi(l, 0, J_AV + 1)
                act.wait_ge(chunk_done, after(nth(l, 0, J_LAT + 2)))
                act.activation(tmp1[:], bank(2), ACT.Square).then_inc(lat_squared, 1)
                hi(l, 0, J_AV + 2)
                act.wait_ge(chunk_done, after(nth(l, 0, J_LAT + 3)))
                act.activation(sq_kr[:], bank(3), ACT.Square).then_inc(lat_squared, 1)
                hi(l, 0, J_AV + 3)
                for g in range(G - 1):
                    act.wait_ge(chunk_done, after(nth(l, 0, J_AV + g)))
                    act.activation(tile(av_t, g), bank(6 + g % 2), ACT.Copy).then_inc(av_taken, 1)
                    if g == 0:
                        act.wait_ge(lat_total, after(l))
                        act.activation(small[:, 0:4], ps[:, 4 * 512:4 * 512 + 4], ACT.Sqrt, bias=eps[:],
                                       scale=1.0 / (2 * P))
                        act.activation(small[:, 4:8], ps[:, 4 * 512 + 4:4 * 512 + 8], ACT.Sqrt, bias=eps[:],
                                       scale=1.0 / P).then_inc(lat_root, 1)
                    hi(l, 0, J_AV + g + 4)

                def take_bx(quads, j, n, b=0):
                    act.wait_ge(chunk_done, after(nth(l, quads, j)))
                    act.wait_ge(pooled, after(n - 1))
                    act.activation(bx[:], bank(b), ACT.Copy).then_inc(bx_taken, 1)

                def squares(n):
                    act.wait_ge(c_ready, after(n * 4))
                    act.activation(qn_hi[:], bank(5), ACT.Copy, scale=col("qn")).then_inc(qn_hi_made, 1)
                    act.wait_ge(c_ready, after(n * 4 + 1))
                    act.activation(qr_gained[:], bank(6), ACT.Copy, scale=col("qr")).then_inc(qr_scaled, 1)
                    for b, o in ((5, sq_a), (6, sq_b), (7, sq_k)):
                        act.wait_ge(c_ready, after(n * 4 + (b - 5)))
                        act.activation(o[:], bank(b), ACT.Square).then_inc(c_squared, 1)

                def roots(n):
                    act.wait_ge(stat_ready, after(n))
                    act.activation(small[:, 0:8], ps[:, 4 * 512:4 * 512 + 8], ACT.Sqrt, bias=eps[:],
                                   scale=1.0 / QK).then_inc(c_root, 1)

                def v_hi(n):
                    act.wait_ge(c_ready, after(n * 4 + 3))
                    act.activation(cv_hi[:], bank(1), ACT.Copy).then_inc(cv_hi_made, 1)

                def bz_gate(quads, j):
                    act.wait_ge(chunk_done, after(nth(l, quads, j)))
                    act.activation(sz_b[:], bank(0), ACT.Tanh, scale=0.5).then_inc(bz_tanh, 1)

                def exponentials(n):
                    for k, blocks in enumerate(((3,), (2, 0), (1,))):
                        act.wait_ge(s_max, after(n * 3 + k))
                        for b in blocks:
                            s = slice(ROW_AT[b], ROW_AT[b] + (b + 1) * P)
                            last = act.activation(prob[:, s], ps[:, SC + s.start:SC + s.stop], ACT.Exp,
                                                  bias=small[:, 28 + b:29 + b], scale=small[:, 16 + b:17 + b],
                                                  accum_out=small[:, 32 + b:33 + b])
                        last.then_inc(exp_made, 1)

                def pt_split_hi(n):
                    act.wait_ge(pt_ready, after(n))
                    for i, w in ((0, 512), (512, 512), (1024, 256)):
                        act.activation(pt_hi[:, i:i + w], ps[:, SC + i:SC + i + w], ACT.Copy).then_inc(pt_hi_made, 1)

                first = l * G
                take_bx(0, J_H0, first, 3)
                squares(first)
                v_hi(first)
                hi(l, 0, J_H0 + 4)
                roots(first)
                act.wait_ge(chunk_done, after(nth(l, 0, J_H0 + 2)))
                act.activation(tile(av_t, G - 1), bank(3), ACT.Copy).then_inc(av_taken, 1)
                hi(l, 0, J_H0 + 5)
                bz_gate(0, J_H0 + 3)
                with act.Fori(0, G - 1) as g:
                    n = l * G + g
                    following = l * G + 1 + g
                    exponentials(n)
                    hi(l, g, J_H1 + 2)
                    hi(l, g, J_H1 + 3)
                    take_bx(g, J_H1, following)
                    pt_split_hi(n)
                    squares(following)
                    hi(l, g, J_H1 + 4)
                    act.wait_ge(cz_ready, after(l * (G - 1) + g))
                    act.activation(sz_c[:], bank(0), ACT.Tanh, scale=0.5).then_inc(cz_tanh, 1)
                    roots(following)
                    act.wait_ge(oc_ready, after(n))
                    v_hi(following)
                    hi(l, g, J_H1 + 5)
                    bz_gate(g, J_H1 + 3)
                final = l * G + (G - 1)
                exponentials(final)
                hi(l, 0, J_M1 + 1)
                hi(l, 0, J_M1 + 2)
                act.wait_ge(chunk_done, after(nth(l, 0, J_CZ)))
                act.activation(sz_c[:], bank(0), ACT.Tanh, scale=0.5).then_inc(cz_tanh, 1)
                pt_split_hi(final)

                act.wait_ge(act1_made, after(l * G + (G - 1)))
                act.dma_start(rows[:], rows_in[l].partition_broadcast(P)).then_inc(rows_loaded, 16)
                act.wait_ge(ln_var, after(l))
                act.activation(small[:, 8:12], small[:, 4:8], ACT.Sqrt, bias=eps[:]).then_inc(ln_root, 1)

                def merge(half, j_at):
                    with act.Fori(0, 2) as i:
                        for u in range(4):
                            q = l * (2 * KD) + i * 4 + (half * KD + u)
                            act.wait_ge(m_done, after(q - 2))
                            for branch in range(2):
                                act.wait_ge(chunk_done, after(nth(l, i * 3, j_at + 3 * u + branch)))
                                act.activation(th[:, 2 * (u % 2) + branch, :], bank(4 * (1 - u % 2) + branch), ACT.Tanh,
                                               scale=0.5).then_inc(g_tanh, 1)
                                hi(l, i * 3, j_at + 3 * u + branch + 3)
                            act.wait_ge(chunk_done, after(nth(l, i * 3, j_at + 3 * u + 2)))
                            hi(l, i * 3, j_at + 3 * u + 5)

                merge(0, J_M1)

                act.wait_ge(chunk_done, after(nth(l, 0, J_MIX)))
                hi(l, 0, J_MIX + 3)

                with act.Fori(0, 2) as i:
                    for u in range(2):
                        n = l * G + i * 2 + u
                        j = J_H2 + 6 * u
                        step = Steps(act_steps, n * 6, 6)
                        act.wait_ge(act2_made, after(n - 1))
                        act.wait_ge(chunk_done, after(nth(l, i * 3, j)))
                        hi(l, i * 3, j + 3)
                        act.wait_ge(chunk_done, after(nth(l, i * 3, j + 1)))
                        act.activation(dk_hi[:], bank(1), ACT.Copy).then_inc(dk_hi_made, 1)
                        hi(l, i * 3, j + 4)
                        act.wait_ge(chunk_done, after(nth(l, i * 3, j + 2)))
                        act.activation(dv_t[:], bank(0), ACT.Copy).then_inc(dv_taken, 1)
                        hi(l, i * 3, j + 5)
                        act.wait_ge(z_ready, after(n))
                        pieces = ((0, 512), (512, 1024), (1024, TRI))
                        magnitudes, exps = [], []
                        for a, b in pieces:
                            act.activation(z_s[:, a:b], ps[:, SC + a:SC + b], ACT.Abs).then_inc(step.done, 1)
                            magnitudes.append(step.next())
                        for (a, b), k in zip(pieces, magnitudes):
                            act.wait_ge(step.done, k)
                            act.activation(z_s[:, a:b], z_s[:, a:b], ACT.Exp, scale=-1.0).then_inc(step.done, 1)
                            exps.append(step.next())
                        for (a, b), k in zip(pieces, exps):
                            act.wait_ge(step.done, k)
                            act.activation(z_s[:, a:b], z_s[:, a:b], ACT.Ln, bias=1.0).then_inc(z_log, 1)
                        act.wait_ge(chunk_done, after(nth(l, i * 3, j + 3)))
                        act.activation(a_u[:], bank(1), ACT.Copy).then_inc(au_taken, 1)
                        hi(l, i * 3, j + 6)
                        act.wait_ge(dvt_ready, after(n))
                        act.activation(dv_hi[:], bank(5), ACT.Copy).then_inc(dv_hi_made, 1)
                        act.wait_ge(chunk_done, after(nth(l, i * 3, j + 4)))
                        act.activation(sz_a[:], bank(0), ACT.Tanh, scale=0.5).then_inc(az_tanh, 1)
                        hi(l, i * 3, j + 7)
                        act.wait_ge(cum_ready, after(n))
                        for a, b in pieces:
                            act.activation(sp[:, a:b], ps[:, SC + a:SC + b], ACT.Exp).then_inc(a_made, 1)
                        act.wait_ge(chunk_done, after(nth(l, i * 3, j + 5)))
                        act.activation(sz_d[:], bank(1), ACT.Tanh, scale=0.5).then_inc(dz_tanh, 1)
                        hi(l, i * 3, j + 8)
                        step.close()

                act.wait_ge(act2_made, after(l * G + (G - 1)))
                act.dma_start(p_raw[:], p_in[l]).then_inc(p_loaded, 16)
                merge(1, J_M2)

                with act.Fori(0, 2) as i:
                    for u in range(4):
                        n = l * KD + i * 4 + u
                        act.wait_ge(chunk_done, after(nth(l, i, J_WO + u)))
                        hi(l, i, J_WO + u + 3)
                        act.wait_ge(x_moved, after(n))
                        act.wait_ge(o_summed, after(n - 2))
                        act.activation(o_sq[:, u % 2, :], tile(x, i * 4 + u), ACT.Square).then_inc(o_squared, 1)
                for d in range(KD):
                    if d % 4 == 3:
                        act.wait_ge(chunk_done, after(nth(l, 0, J_PLE + d // 4)))
                    else:
                        act.wait_ge(e_ready, after(l * (KD - 2) + (d - d // 4)))
                    act.activation(tile(e, d), bank(2 + d % 2), ACT.Copy).then_inc(e_taken, 1)
                    if d % 4 == 3:
                        hi(l, 0, J_PLE + d // 4 + 3)
                act.wait_ge(o_total, after(l))
                act.activation(o_r[:], bank(6), ACT.Sqrt, bias=eps[:], scale=1.0 / D_MODEL).then_inc(o_root, 1)
                for d in range(KD):
                    if d:
                        act.wait_ge(x_made, after(l * KD + (d - 1)))
                        square(d - 1)
                    act.wait_ge(gate_scaled, after(l * KD + d))
                    if J_GATE + d + 3 < CHUNKS:
                        hi(l, 0, J_GATE + d + 3)
                    act.activation(o_t[:, d % 2, :], o_t[:, d % 2, :], ACT.Tanh, scale=0.5).then_inc(gate_tanh, 1)
                act.wait_ge(x_made, after(l * KD + (KD - 1)))
                square(KD - 1)

        @block.vector
        def _(dve):
            for s in given["dve"]:
                dve.sem_inc(s, CREDIT)

            def low(o, src, hi_part):
                return dve.tensor_tensor(o, src, hi_part.bitcast(F32), ALU.subtract)

            def split(step, o_hi, o_lo, src):
                dve.tensor_copy(o_hi, src).then_inc(step.done, 1)
                dve.wait_ge(step.done, step.next())
                return low(o_lo, src, o_hi)

            def tile_at(t, start):
                return t[:, start:start + SEQ] if isinstance(start, int) else t[:, bass.ds(start, SEQ)]

            def rotate(step, o, t, scratch):
                half = ROPE // 2
                dve.tensor_tensor(o, t, cos_t[:], ALU.mult).then_inc(step.done, 1)
                dve.wait_ge(step.done, step.next())
                dve.tensor_tensor(scratch[0:half, :], t[half:ROPE, :], sin_t[half:ROPE, :], ALU.mult).then_inc(
                    step.done, 1)
                dve.wait_ge(step.done, step.next())
                dve.tensor_tensor(scratch[half:ROPE, :], t[0:half, :], sin_t[0:half, :], ALU.mult).then_inc(
                    step.done, 1)
                dve.wait_ge(step.done, step.next())
                dve.tensor_tensor(o[0:ROPE, :], o[0:ROPE, :], scratch[0:ROPE, :], ALU.add).then_inc(step.done, 1)
                dve.wait_ge(step.done, step.next())

            def steps(phase, n):
                return Steps(own[phase], n * STEPS[phase], STEPS[phase])

            step = steps("start", 0)
            dve.memset(eps[:], EPS)
            dve.wait_ge(const_loaded, 16)
            for t, name in ((ident, "ident"), (ones, "ones"), (negtri, "negtri"), (neg_i, "neg_i"), (mask_c, "mask_c"),
                            (keep, "keep"), (inv_edge, "inv_edge"), (inv_win, "inv_win")):
                dve.tensor_copy(t[:], c_st[:, CC[name]])
            dve.tensor_scalar(negones[:], c_st[:, CC["ones"]], -1.0, None, ALU.mult)
            dve.tensor_copy(mask_d[:], c_st[:, CC["mask_d"]]).then_inc(consts_made, 1)
            dve.wait_ge(pos_loaded, 16)
            dve.tensor_copy(turns[:], pos_i[:]).then_inc(step.done, 1)
            dve.wait_ge(step.done, step.next())
            dve.tensor_scalar(ang[:], turns[:], c_st[:, CC["freq"]], None, ALU.mult).then_inc(step.done, 1)
            dve.wait_ge(step.done, step.next())
            dve.tensor_scalar(turns[:], ang[:], float(1 / (2 * np.pi)), None, ALU.mult).then_inc(step.done, 1)
            dve.wait_ge(step.done, step.next())
            dve.tensor_scalar(turns[:], turns[:], ROUND, None, ALU.add).then_inc(step.done, 1)
            dve.wait_ge(step.done, step.next())
            dve.tensor_scalar(turns[:], turns[:], ROUND, None, ALU.subtract).then_inc(step.done, 1)
            dve.wait_ge(step.done, step.next())
            for part in TWO_PI:
                dve.scalar_tensor_tensor(ang[:], turns[:], -part, ang[:], ALU.mult, ALU.add).then_inc(step.done, 1)
                dve.wait_ge(step.done, step.next())
            dve.tensor_scalar(ang[:], ang[:], PI_IN, -PI_IN, ALU.min, ALU.max).then_inc(step.done, 1)
            dve.wait_ge(step.done, step.next())
            dve.tensor_scalar(turns[:], ang[:], -1.0, None, ALU.mult).then_inc(step.done, 1)
            dve.wait_ge(step.done, step.next())
            dve.tensor_tensor(turns[:], turns[:], ang[:], ALU.max).then_inc(step.done, 1)
            dve.wait_ge(step.done, step.next())
            dve.tensor_scalar(turns[:], turns[:], -1.0, float(np.pi / 2), ALU.mult, ALU.add).then_inc(rope_args, 1)
            dve.wait_ge(rope_sines, after(0))
            dve.tensor_scalar(sin_t[ROPE // 2:ROPE, :], sin_t[ROPE // 2:ROPE, :], -1.0, None, ALU.mult).then_inc(
                step.done, 1)
            dve.wait_ge(step.done, step.next())
            step.close()
            def add_square(d, n):
                dve.wait_ge(n_squared, after(n))
                dve.tensor_tensor(n_acc[:], n_acc[:], tile(n_sq, d), ALU.add).then_inc(n_summed, 1)
                dve.wait_ge(n_summed, after(n))

            def diagonal(o, inverse):
                return dve.tensor_tensor(o[:].rearrange("p (t s) -> p t s", t=TB),
                                         ident[:].unsqueeze(1).broadcast_to([P, TB, P]),
                                         inverse.unsqueeze(2).broadcast_to([P, TB, P]), ALU.mult)

            dve.wait_ge(par_loaded, 16)

            with dve.Fori(0, DEPTH) as l:
                step = steps("norm", l)
                dve.tensor_copy(par[:], par_all[:, bass.ds(l * PARAMS, PARAMS)]).then_inc(step.done, 1)
                dve.wait_ge(step.done, step.next())
                dve.wait_ge(n_root, after(l))
                dve.reciprocal(small[:, 4:8], small[:, 0:4]).then_inc(step.done, 1)
                dve.wait_ge(step.done, step.next())
                diagonal(n_r, small[:, 4:8]).then_inc(n_diag, 1)
                step.close()
                dve.wait_ge(n_spread, after(l))
                for k in range(KD + 1):
                    if k < KD:
                        dve.scalar_tensor_tensor(n_t[:, k % 2, :], tile(x, k), col("norm", k), bank(6), ALU.mult,
                                                 ALU.mult).then_inc(n_scaled, 1)
                        dve.wait_ge(n_scaled, after(l * KD + k))
                    if k:
                        dve.wait_ge(n_hi_made, after(l * KD + (k - 1)))
                        low(tile(h_lo, k - 1), n_t[:, (k - 1) % 2, :], tile(h_hi, k - 1)).then_inc(h_made, 1)
                        dve.wait_ge(h_made, after(l * KD + (k - 1)))

                step = steps("latents", l)
                dve.memset(cs_pad[:, 0:PAD], 0.0).then_inc(step.done, 1)
                dve.wait_ge(step.done, step.next())
                dve.wait_ge(lat_squared, after(l * 4 + 1))
                dve.tensor_tensor(sq_a[:], sq_a[:], sq_b[:], ALU.add).then_inc(lat_summed, 1)
                dve.wait_ge(lat_summed, after(l))
                dve.wait_ge(lat_squared, after(l * 4 + 3))
                dve.tensor_scalar(tmp0[:], bank(3), col("kr"), None, ALU.mult).then_inc(kr_taken, 1)
                dve.wait_ge(kr_taken, after(l))
                rotate(step, krr[:], tmp0[:], prob[:, 0:SEQ])
                dve.wait_ge(lat_root, after(l))
                dve.reciprocal(small[:, 8:16], small[:, 0:8]).then_inc(step.done, 1)
                dve.wait_ge(step.done, step.next())
                diagonal(sq_b, small[:, 8:12])
                diagonal(r_k, small[:, 12:16]).then_inc(lat_diag, 1)
                dve.wait_ge(lat_spread, after(l))
                dve.tensor_copy(r_k[:], bank(4))
                dve.tensor_copy(sq_b[:], bank(5)).then_inc(step.done, 1)
                dve.wait_ge(step.done, step.next())
                for k in range(2):
                    dve.scalar_tensor_tensor(tmp0[:], bank(k), col("cq", k), sq_b[:], ALU.mult, ALU.mult).then_inc(
                        step.done, 1)
                    dve.wait_ge(step.done, step.next())
                    split(step, cqn_hi[:, k, :], cqn_lo[:, k, :], tmp0[:]).then_inc(step.done, 1)
                    dve.wait_ge(step.done, step.next())
                dve.scalar_tensor_tensor(tmp0[:], bank(2), col("ckv"), r_k[:], ALU.mult, ALU.mult).then_inc(
                    step.done, 1)
                dve.wait_ge(step.done, step.next())
                split(step, ckvn_hi[:], ckvn_lo[:], tmp0[:]).then_inc(lat_made, 1)
                value = dve.to_reg(after(l))
                dve.wait_ge(const_loaded, 16)
                dve.wait_ge(lat_made, value)
                step.close()

                def window_sums(step, n, head):
                    back = PAD - (2 << head)
                    if not isinstance(back, int):
                        dve.compute_val(back)
                    dve.wait_ge(bx_taken, after(n))
                    dve.tensor_tensor_scan(cs_pad[:, PAD:], ones[:, 0:1].to_broadcast([P, SEQ]), bx[:], 0.0, ALU.mult,
                                           ALU.add).then_inc(step.done, 1)
                    dve.wait_ge(step.done, step.next())
                    dve.tensor_tensor(diff[:], cs_pad[:, PAD:], tile_at(cs_pad, back), ALU.subtract).then_inc(
                        step.done, 1)
                    dve.wait_ge(step.done, step.next())
                    dve.tensor_tensor(edge[:], diff[:, 0:PAD], tile(inv_edge, head, PAD), ALU.mult).then_inc(
                        step.done, 1)
                    dve.wait_ge(step.done, step.next())
                    dve.scalar_tensor_tensor(diff[:], diff[:], tile(inv_win, head, 1), bx[:], ALU.mult,
                                             ALU.subtract).then_inc(step.done, 1)
                    dve.wait_ge(step.done, step.next())
                    dve.tensor_tensor(diff[:, 0:PAD], edge[:], bx[:, 0:PAD], ALU.subtract).then_inc(step.done, 1)
                    dve.wait_ge(step.done, step.next())
                    split(step, pool_hi[:], pool_lo[:], diff[:]).then_inc(pooled, 1)
                    dve.wait_ge(pooled, after(n))

                def q_parts(step, n):
                    dve.wait_ge(qn_hi_made, after(n))
                    dve.wait_ge(c_squared, after(n * 3))
                    dve.scalar_tensor_tensor(qn_lo[:], bank(5), col("qn"), qn_hi[:].bitcast(F32), ALU.mult,
                                             ALU.subtract).then_inc(qn_taken, 1)
                    dve.wait_ge(qn_taken, after(n))

                def k_squares(n):
                    dve.wait_ge(c_squared, after(n * 3 + 2))
                    dve.tensor_tensor(sq_k[:], sq_k[:], sq_kr[:], ALU.add).then_inc(sqk_made, 1)
                    dve.wait_ge(sqk_made, after(n))

                def q_rotary(step, n):
                    dve.wait_ge(c_squared, after(n * 3 + 1))
                    dve.wait_ge(qr_scaled, after(n))
                    rotate(step, tmp1[:], qr_gained[:], r_k[:])
                    split(step, qr_hi[:], qr_lo[:], tmp1[:]).then_inc(q_made, 1)
                    dve.wait_ge(q_made, after(n))

                def inverses(step, n):
                    dve.wait_ge(c_root, after(n))
                    dve.reciprocal(small[:, 8:16], small[:, 0:8]).then_inc(step.done, 1)
                    dve.wait_ge(step.done, step.next())
                    diagonal(r_k, small[:, 12:16]).then_inc(rk_made, 1)
                    dve.wait_ge(rk_made, after(n))
                    dve.tensor_scalar(small[:, 16:20], small[:, 8:12], Q_SCALE_C, None, ALU.mult).then_inc(
                        step.done, 1)
                    dve.wait_ge(step.done, step.next())
                    dve.tensor_scalar(small[:, 20:24], small[:, 8:12], -Q_SCALE_C, None, ALU.mult).then_inc(
                        step.done, 1)
                    dve.wait_ge(step.done, step.next())

                def v_lo(n):
                    dve.wait_ge(cv_hi_made, after(n))
                    low(cv_lo[:], bank(1), cv_hi[:]).then_inc(cv_made, 1)
                    dve.wait_ge(cv_made, after(n))

                def k_parts(step, n):
                    dve.wait_ge(rk_ready, after(n))
                    dve.tensor_copy(tmp1[:], bank(6)).then_inc(step.done, 1)
                    dve.wait_ge(step.done, step.next())
                    dve.scalar_tensor_tensor(tmp0[:], bank(7), col("kn"), tmp1[:], ALU.mult, ALU.mult).then_inc(
                        step.done, 1)
                    dve.wait_ge(step.done, step.next())
                    dve.tensor_tensor(tmp1[:], krr[:], tmp1[:], ALU.mult).then_inc(step.done, 1)
                    dve.wait_ge(step.done, step.next())
                    dve.tensor_copy(kn_hi[:], tmp0[:]).then_inc(step.done, 1)
                    dve.wait_ge(step.done, step.next())
                    dve.tensor_copy(kr_hi[:], tmp1[:]).then_inc(step.done, 1)
                    dve.wait_ge(step.done, step.next())
                    low(kn_lo[:], tmp0[:], kn_hi[:]).then_inc(step.done, 1)
                    dve.wait_ge(step.done, step.next())
                    low(kr_lo[:], tmp1[:], kr_hi[:]).then_inc(k_made, 1)
                    dve.wait_ge(k_made, after(n))

                def pool_scale(quads, j, n, head):
                    dve.wait_ge(chunk_done, after(nth(l, quads, j)))
                    pool_gain = tile(par, head + PC["pool"].start, 1)
                    dve.tensor_scalar(diff[:], bank(2), pool_gain, None,
                                      ALU.mult).then_inc(pool_taken, 1)
                    dve.wait_ge(pool_taken, after(n))

                def bz_gate(n):
                    dve.wait_ge(bz_tanh, after(n))
                    dve.scalar_tensor_tensor(sz_b[:], sz_b[:], 1.0, bank(0), ALU.add, ALU.mult).then_inc(bz_taken, 1)
                    dve.wait_ge(bz_taken, after(n))

                def gated_b(step, head):
                    dve.scalar_tensor_tensor(tmp0[:], diff[:], 0.5, sz_b[:], ALU.mult, ALU.mult).then_inc(step.done, 1)
                    dve.wait_ge(step.done, step.next())
                    split(step, tile(act_hi, head), tile(act_lo, head), tmp0[:]).then_inc(step.done, 1)
                    dve.wait_ge(step.done, step.next())

                groups = ((3,), (2, 0), (1,))

                def maxima(step, n):
                    for k, blocks in enumerate(groups):
                        dve.wait_ge(s_ready, after(n * 3 + k))
                        for b in blocks:
                            s = SC + ROW_AT[b]
                            dve.tensor_reduce(small[:, 24 + b:25 + b], ps[:, s:s + (b + 1) * P],
                                              mybir.AxisListType.X, ALU.max).then_inc(step.done, 1)
                            dve.wait_ge(step.done, step.next())
                            last = dve.tensor_tensor(small[:, 28 + b:29 + b], small[:, 24 + b:25 + b],
                                                     small[:, 20 + b:21 + b], ALU.mult)
                        last.then_inc(s_max, 1)
                    dve.wait_ge(s_max, after(n * 3 + 2))

                def probabilities(step, n):
                    for k, blocks in enumerate(groups):
                        dve.wait_ge(exp_made, after(n * 3 + k))
                        for b in blocks:
                            s = slice(ROW_AT[b], ROW_AT[b] + (b + 1) * P)
                            dve.reciprocal(small[:, 36 + b:37 + b], small[:, 32 + b:33 + b]).then_inc(step.done, 1)
                            dve.wait_ge(step.done, step.next())
                            last = dve.tensor_scalar(prob[:, s], prob[:, s], small[:, 36 + b:37 + b], None, ALU.mult)
                    last.then_inc(p_made, 1)

                def pt_split_lo(n):
                    for k, (i, w) in enumerate(((0, 512), (512, 512), (1024, 256))):
                        dve.wait_ge(pt_hi_made, after(n * 3 + k))
                        last = low(pt_lo[:, i:i + w], ps[:, SC + i:SC + i + w], pt_hi[:, i:i + w])
                    last.then_inc(pt_made, 1)

                def cz_gate(n):
                    dve.wait_ge(cz_tanh, after(n))
                    dve.scalar_tensor_tensor(sz_c[:], sz_c[:], 1.0, bank(0), ALU.add, ALU.mult).then_inc(cz_taken, 1)
                    dve.wait_ge(cz_taken, after(n))

                def branch_c(step, n, head):
                    dve.wait_ge(oc_ready, after(n))
                    dve.scalar_tensor_tensor(tmp0[:], bank(5), 0.5, sz_c[:], ALU.mult, ALU.mult).then_inc(step.done, 1)
                    dve.wait_ge(step.done, step.next())
                    split(step, tile(act_hi, head + G), tile(act_lo, head + G), tmp0[:]).then_inc(act1_made, 1)
                    dve.wait_ge(act1_made, after(n))

                first = l * G
                front = steps("front", first)
                q_parts(front, first)
                k_squares(first)
                q_rotary(front, first)
                inverses(front, first)
                window_sums(front, first, 0)
                v_lo(first)
                k_parts(front, first)
                pool_scale(0, J_H0 + 2, first, 0)
                front.close()
                dve.wait_ge(bz_tanh, after(first))
                dve.scalar_tensor_tensor(sz_b[:], sz_b[:], 1.0, bank(0), ALU.add, ALU.mult).then_inc(bz_taken, 1)
                value = dve.to_reg(after(first))
                dve.wait_ge(const_loaded, 16)
                dve.wait_ge(bz_taken, value)
                with dve.Fori(0, G - 1) as g:
                    n = l * G + g
                    following = l * G + 1 + g
                    front, own_back = steps("front", following), steps("back", n)
                    maxima(own_back, n)
                    probabilities(own_back, n)
                    gated_b(own_back, g)
                    pt_split_lo(n)
                    q_parts(front, following)
                    window_sums(front, following, g + 1)
                    k_squares(following)
                    q_rotary(front, following)
                    inverses(front, following)
                    cz_gate(n)
                    k_parts(front, following)
                    pool_scale(g, J_H1 + 2, following, g + 1)
                    branch_c(own_back, n, g)
                    v_lo(following)
                    bz_gate(following)
                    front.close()
                    own_back.close()
                final = l * G + (G - 1)
                last_head = steps("back", final)
                maxima(last_head, final)
                probabilities(last_head, final)
                gated_b(last_head, G - 1)
                cz_gate(final)
                pt_split_lo(final)
                branch_c(last_head, final, G - 1)
                last_head.close()

                step = steps("ln", l)
                for t in range(TB):
                    dve.wait_ge(ln_ready, after(l * TB + t))
                    dve.bn_stats(small[:, 12 + 6 * t:18 + 6 * t], bank(t)).then_inc(step.done, 1)
                    value = dve.to_reg(step.next())
                    dve.wait_ge(const_loaded, 16)
                    dve.wait_ge(step.done, value)
                    dve.bn_aggr(small[:, 36:38], small[:, 12 + 6 * t:18 + 6 * t]).then_inc(step.done, 1)
                    dve.wait_ge(step.done, step.next())
                    dve.tensor_copy(small[:, t:t + 1], small[:, 36:37])
                    last = dve.tensor_copy(small[:, 4 + t:5 + t], small[:, 37:38])
                    if t < TB - 1:
                        last.then_inc(step.done, 1)
                        dve.wait_ge(step.done, step.next())
                last.then_inc(ln_var, 1)
                dve.wait_ge(ln_root, after(l))
                dve.reciprocal(small[:, 12:16], small[:, 8:12]).then_inc(step.done, 1)
                dve.wait_ge(step.done, step.next())
                for t in range(TB):
                    dve.tensor_scalar(xh[:, t, :], bank(t), small[:, t:t + 1], small[:, 12 + t:13 + t], ALU.subtract,
                                      ALU.mult).then_inc(ln_taken, 1)
                dve.wait_ge(rows_loaded, (l + 1) * 16)
                for t in range(TB):
                    dve.wait_ge(ln_taken, after(l * TB + t))
                    dve.tensor_tensor(xh[:, t, :], xh[:, t, :], rows[:, 0, :], ALU.mult).then_inc(step.done, 1)
                    dve.wait_ge(step.done, step.next())
                    dve.tensor_tensor(xh[:, t, :], xh[:, t, :], rows[:, 1, :], ALU.add).then_inc(step.done, 1)
                    dve.wait_ge(step.done, step.next())
                    last = split(step, tile(vn_hi, t), tile(vn_lo, t), xh[:, t, :])
                last.then_inc(ln_made, 1)
                value = dve.to_reg(after(l))
                dve.wait_ge(const_loaded, 16)
                dve.wait_ge(ln_made, value)
                step.close()

                def merge(half, j_at):
                    with dve.Fori(0, 2) as i:
                        phase = f"merge{half}"
                        step = Steps(own[phase], l * 2 * STEPS[phase] + i * STEPS[phase], STEPS[phase])
                        for u in range(4):
                            q = l * (2 * KD) + i * 4 + (half * KD + u)
                            d = i * 4 + u
                            b = 4 * (1 - u % 2) + 2
                            dve.wait_ge(g_tanh, after(q * 2 + 1))
                            dve.wait_ge(y_ready, after(q))
                            dve.scalar_tensor_tensor(m_part[:, 0, :], th[:, 2 * (u % 2), :], 1.0, bank(b), ALU.add,
                                                       ALU.mult).then_inc(step.done, 1)
                            dve.wait_ge(step.done, step.next())
                            dve.wait_ge(chunk_done, after(nth(l, i * 3, j_at + 3 * u + 2)))
                            dve.scalar_tensor_tensor(m_part[:, 1, :], th[:, 2 * (u % 2) + 1, :], 1.0, bank(b + 1),
                                                     ALU.add, ALU.mult).then_inc(step.done, 1)
                            dve.wait_ge(step.done, step.next())
                            if half == 0:
                                dve.tensor_tensor(tile(merged, d), m_part[:, 0, :], m_part[:, 1, :],
                                                  ALU.add).then_inc(m_done, 1)
                                dve.wait_ge(m_done, after(q))
                            else:
                                dve.tensor_tensor(m_part[:, 0, :], m_part[:, 0, :], m_part[:, 1, :], ALU.add).then_inc(
                                    step.done, 1)
                                dve.wait_ge(step.done, step.next())
                                dve.tensor_tensor(m_part[:, 0, :], m_part[:, 0, :], tile(merged, d), ALU.add).then_inc(
                                    step.done, 1)
                                dve.wait_ge(step.done, step.next())
                                dve.tensor_scalar(tile(m_hi, d), m_part[:, 0, :], 0.5, None, ALU.mult).then_inc(
                                    step.done, 1)
                                dve.wait_ge(step.done, step.next())
                                dve.scalar_tensor_tensor(tile(m_lo, d), m_part[:, 0, :], 0.5,
                                                         tile(m_hi, d).bitcast(F32), ALU.mult,
                                                         ALU.subtract).then_inc(m_done, 1)
                                dve.wait_ge(m_done, after(q))
                        step.close()

                merge(0, J_M1)

                for g in range(G):
                    if g < G - 1:
                        dve.wait_ge(mix_ready, after(l * (G - 1) + g))
                    else:
                        dve.wait_ge(chunk_done, after(nth(l, 0, J_MIX)))
                    bias = rows[:, 2, g * P:(g + 1) * P].unsqueeze(1).broadcast_to([P, TB, P])
                    dve.tensor_tensor(tile(mix_t, g).rearrange("p (t s) -> p t s", t=TB),
                                      bank(4 + g).rearrange("p (t s) -> p t s", t=TB), bias,
                                      ALU.add).then_inc(mix_taken, 1)
                    value = dve.to_reg(after(l * G + g))
                    dve.wait_ge(const_loaded, 16)
                    dve.wait_ge(mix_taken, value)

                with dve.Fori(0, 2) as i:
                    for u in range(2):
                        g = i * 2 + u
                        n = l * G + i * 2 + u
                        j = J_H2 + 6 * u
                        step = steps("half2", n)
                        dve.wait_ge(chunk_done, after(nth(l, i * 3, j)))
                        dve.tensor_scalar(dq_hi[:], bank(0), Q_SCALE_D, None, ALU.mult).then_inc(step.done, 1)
                        dve.wait_ge(step.done, step.next())
                        dve.scalar_tensor_tensor(dq_lo[:], bank(0), Q_SCALE_D, dq_hi[:].bitcast(F32), ALU.mult,
                                                 ALU.subtract).then_inc(dq_made, 1)
                        dve.wait_ge(dq_made, after(n))
                        dve.wait_ge(dk_hi_made, after(n))
                        low(dk_lo[:], bank(1), dk_hi[:]).then_inc(dk_made, 1)
                        dve.wait_ge(dk_made, after(n))
                        for k, (a, b) in enumerate(((0, 512), (512, 1024), (1024, TRI))):
                            dve.wait_ge(z_log, after(n * 3 + k))
                            dve.scalar_tensor_tensor(sp[:, a:b], ps[:, SC + a:SC + b], 0.0, z_s[:, a:b], ALU.max,
                                                     ALU.add).then_inc(step.done, 1)
                            dve.wait_ge(step.done, step.next())
                            last = split(step, s_hi[:, a:b], s_lo[:, a:b], sp[:, a:b])
                            if k < 2:
                                last.then_inc(step.done, 1)
                                dve.wait_ge(step.done, step.next())
                        last.then_inc(sp_made, 1)
                        dve.wait_ge(sp_made, after(n))
                        dve.wait_ge(dv_hi_made, after(n))
                        low(dv_lo[:], bank(5), dv_hi[:]).then_inc(dv_made, 1)
                        dve.wait_ge(dv_made, after(n))
                        dve.wait_ge(az_tanh, after(n))
                        dve.scalar_tensor_tensor(sz_a[:], sz_a[:], 1.0, bank(0), ALU.add, ALU.mult).then_inc(
                            az_taken, 1)
                        dve.wait_ge(az_taken, after(n))
                        dve.wait_ge(mix_taken, after(l * G + (G - 1)))
                        dve.tensor_tensor(tmp2[:], tile(mix_t, g), a_u[:], ALU.mult).then_inc(step.done, 1)
                        dve.wait_ge(step.done, step.next())
                        dve.scalar_tensor_tensor(tmp2[:], tmp2[:], 0.5, sz_a[:], ALU.mult, ALU.mult).then_inc(
                            step.done, 1)
                        dve.wait_ge(step.done, step.next())
                        split(step, tile(act_hi, g), tile(act_lo, g), tmp2[:]).then_inc(step.done, 1)
                        dve.wait_ge(step.done, step.next())
                        for k, (a, b) in enumerate(((0, 512), (512, 1024), (1024, TRI))):
                            dve.wait_ge(a_made, after(n * 3 + k))
                            last = split(step, s_hi[:, a:b], s_lo[:, a:b], sp[:, a:b])
                            if k < 2:
                                last.then_inc(step.done, 1)
                                dve.wait_ge(step.done, step.next())
                        last.then_inc(a_split, 1)
                        dve.wait_ge(a_split, after(n))
                        dve.wait_ge(dz_tanh, after(n))
                        dve.scalar_tensor_tensor(sz_d[:], sz_d[:], 1.0, bank(1), ALU.add, ALU.mult).then_inc(
                            dz_taken, 1)
                        dve.wait_ge(dz_taken, after(n))
                        dve.wait_ge(od_ready, after(n))
                        dve.scalar_tensor_tensor(tmp2[:], bank(6), 0.5, sz_d[:], ALU.mult, ALU.mult).then_inc(
                            step.done, 1)
                        dve.wait_ge(step.done, step.next())
                        split(step, tile(act_hi, g + G), tile(act_lo, g + G), tmp2[:]).then_inc(act2_made, 1)
                        dve.wait_ge(act2_made, after(n))
                        step.close()

                merge(1, J_M2)

                step = steps("out", l)
                dve.wait_ge(p_loaded, (l + 1) * 16)
                dve.tensor_copy(p_hi[:], p_raw[:]).then_inc(step.done, 1)
                dve.wait_ge(step.done, step.next())
                low(p_lo[:], p_raw[:], p_hi[:]).then_inc(p_split, 1)
                dve.wait_ge(p_split, after(l))
                dve.memset(o_acc[:], 0.0).then_inc(step.done, 1)
                value = dve.to_reg(step.next())
                dve.wait_ge(const_loaded, 16)
                dve.wait_ge(step.done, value)
                step.close()
                with dve.Fori(0, 2) as i:
                    for u in range(4):
                        d = i * 4 + u
                        n = l * KD + i * 4 + u
                        dve.wait_ge(chunk_done, after(nth(l, i, J_WO + u)))
                        dve.tensor_tensor(tile(x, d), tile(x, d), bank(4 + u % 2), ALU.add).then_inc(x_moved, 1)
                        dve.wait_ge(x_moved, after(n))
                        gain = par[:, bass.ds(d + PC["ple"].start, 1)]
                        dve.tensor_scalar(tile(h_hi, d), tile(x, d), gain, None, ALU.mult).then_inc(hx_hi, 1)
                        dve.wait_ge(hx_hi, after(n))
                        dve.scalar_tensor_tensor(tile(h_lo, d), tile(x, d), gain, tile(h_hi, d).bitcast(F32), ALU.mult,
                                                 ALU.subtract).then_inc(hx_made, 1)
                        dve.wait_ge(hx_made, after(n))
                        dve.wait_ge(o_squared, after(n))
                        dve.wait_ge(o_summed, after(n - 1))
                        dve.tensor_tensor(o_acc[:], o_acc[:], o_sq[:, u % 2, :], ALU.add).then_inc(o_summed, 1)
                        dve.wait_ge(o_summed, after(n))
                dve.wait_ge(o_root, after(l))
                dve.reciprocal(o_r[:], o_r[:]).then_inc(o_inv, 1)
                value = dve.to_reg(after(l))
                dve.wait_ge(const_loaded, 16)
                dve.wait_ge(o_inv, value)

                dve.memset(n_acc[:], 0.0).then_inc(n_zeroed, 1)
                value = dve.to_reg(after(l))
                dve.wait_ge(const_loaded, 16)
                dve.wait_ge(n_zeroed, value)
                with dve.Fori(0, 2) as i:
                    for u in range(5):
                        if u < 4:
                            dve.wait_ge(chunk_done, after(nth(l, i, J_GATE + u)))
                            dve.tensor_tensor(o_t[:, u % 2, :], bank(u % 2), o_r[:], ALU.mult).then_inc(
                                gate_scaled, 1)
                            dve.wait_ge(gate_scaled, after(l * KD + i * 4 + u))
                        if u:
                            d = i * 4 + (u - 1)
                            n = l * KD + i * 4 + (u - 1)
                            t = o_t[:, (u - 1) % 2, :]
                            dve.wait_ge(gate_tanh, after(n))
                            if u == 1:
                                dve.wait_ge(e_taken, after(l * KD + (KD - 1)))
                            dve.scalar_tensor_tensor(t, t, 1.0, tile(e, d), ALU.add, ALU.mult).then_inc(gated, 1)
                            dve.wait_ge(gated, after(n))
                            dve.scalar_tensor_tensor(tile(x, d), t, 0.5, tile(x, d), ALU.mult, ALU.add).then_inc(
                                x_made, 1)
                            dve.wait_ge(x_made, after(n))
                            add_square(d, (l + 1) * KD + i * 4 + (u - 1))


def blocks(w):
    k, n = w.shape
    wide = -(-n // P) * P
    if wide > n:
        w = np.concatenate([w, np.zeros((k, wide - n), w.dtype)], 1)
    return w.reshape(k // P, P, wide // P, P).transpose(0, 2, 1, 3)


def weight_chunks(w, l):
    w_in = w["w_in"][l]

    def part(start, i=0, n=P):
        return list(blocks(w_in[:, start + i * P:start + i * P + n])[:, 0])

    zero = np.zeros((P, P), np.float32)
    outs = {k: blocks(w[k][l]) for k in ("w_a_out", "w_b_out", "w_c_out", "w_d_out", "w_o", "w_ple", "w_ple_gate")}
    w_uq = w["w_uq"][l].reshape(-1, G, QK)
    w_ukv = w["w_ukv"][l].reshape(P, G, 2, P)
    chunks = [part(C_Q, 0), part(C_Q, 1), part(C_KV), part(C_KR, 0, ROPE)]
    chunks += [part(A_V, g) for g in range(G - 1)]

    def head_weights(g):
        qn, qr = blocks(w_uq[:, g, :P]), blocks(w_uq[:, g, P:])
        return [qn[0, 0], qn[1, 0], qr[0, 0], qr[1, 0], w_ukv[:, g, 0], w_ukv[:, g, 1], w["pool_w"][l, g], zero]

    chunks += [part(B_X, 0), head_weights(0), part(A_V, G - 1), part(B_Z, 0)]
    for g in range(G - 1):
        chunks += [part(B_X, g + 1), head_weights(g + 1), part(C_Z, g), part(B_Z, g + 1)]
    chunks.append(part(C_Z, G - 1))

    def merge(a, b, names):
        for d in range(KD):
            chunks.append(part(GATES + a * D_MODEL, d))
            chunks.append(part(GATES + b * D_MODEL, d))
            chunks.append([outs[name][k, d] for name in names for k in range(G)])

    merge(1, 2, ("w_b_out", "w_c_out"))
    chunks.append([w["sgu_w"][l, g].T for g in range(G)] + [zero] * (8 - G))
    for g in range(G):
        chunks += [part(s, g) for s in (D_Q, D_K, D_V, A_U, A_Z, D_Z)]
    merge(0, 3, ("w_a_out", "w_d_out"))
    chunks += [list(outs["w_o"][:, d]) for d in range(KD)]
    chunks += [[outs["w_ple"][k, d] for d in range(4 * i, 4 * i + 4) for k in range(2)] for i in range(2)]
    chunks += [list(outs["w_ple_gate"][:, d]) for d in range(KD)]
    return np.stack([np.stack(c, 1) for c in chunks])


def constants():
    row, col = np.arange(P)[:, None], np.arange(P)[None, :]
    t = np.arange(PAD)
    win = np.array([2 << g for g in range(G)])
    half = ROPE // 2
    freq = (np.float32(10000.0) ** (-np.arange(half, dtype=np.float32) / np.float32(half))).astype(np.float32)
    parts = dict(
        ident=(row == col), ones=np.ones((P, P)), negtri=-1.0 * (row >= col), neg_i=NEG * (row == col),
        mask_c=(col // 64 > row // 64), mask_d=(row >= col),
        keep=(row < P // 2),
        inv_edge=np.tile((1.0 / np.minimum(t[None, :] + 1, win[:, None])).reshape(1, -1), (P, 1)),
        inv_win=np.tile(1.0 / win[None, :], (P, 1)),
        freq=np.concatenate([freq, freq, np.zeros(P - ROPE, np.float32)])[:, None])
    return np.concatenate([np.asarray(parts[k], np.float32) for k in CC], 1)


def kernel(**inputs):
    import concourse.bacc as bacc
    from concourse.bass_utils import run_bass_kernel_spmd

    w = {k: np.asarray(v) for k, v in inputs.items()}

    def by_feature(v):
        n = -(-v.shape[1] // P) * P
        v = np.concatenate([v, np.zeros((DEPTH, n - v.shape[1]), v.dtype)], 1)
        return v.reshape(DEPTH, n // P, P).transpose(2, 0, 1)

    params = np.concatenate([by_feature(v) for v in (
        w["norm_g"], w["ple_norm_g"], w["pool_scale"], w["cq_norm_g"], w["ckv_norm_g"], w["q_norm_g"][:, :P],
        w["q_norm_g"][:, P:], w["k_norm_g"][:, :P], w["k_norm_g"][:, P:])], 2)
    arrays = {
        "x_in": w["x"][0].T.reshape(KD, P, SEQ).transpose(1, 0, 2).reshape(P, KD * SEQ),
        "p_in": w["p"][:, 0].transpose(0, 2, 1).reshape(DEPTH, 2, P, SEQ).transpose(0, 2, 1, 3),
        "pos_in": w["positions"][0],
        "w_in": np.concatenate([weight_chunks(w, l) for l in range(DEPTH)]),
        "par_in": params.reshape(P, DEPTH * PARAMS),
        "rows_in": np.stack([w["ln_v_g"], w["ln_v_b"], w["sgu_b"].reshape(DEPTH, -1)], 1),
        "const_in": constants(),
    }
    arrays = {k: np.ascontiguousarray(v) for k, v in arrays.items()}
    nc = bacc.Bacc("TRN2", target_bir_lowering=False, num_devices=1)
    aps = [nc.dram_tensor(k, v.shape, mybir.dt.from_np(v.dtype), kind="ExternalInput").ap() for k, v in arrays.items()]
    out = nc.dram_tensor("out_x", (P, KD * SEQ), F32, kind="ExternalOutput").ap()
    build(nc, *aps, out)
    r = run_bass_kernel_spmd(nc, [arrays], core_ids=[0])
    y = np.asarray(r.results[0]["out_x"])
    return np.ascontiguousarray(y.reshape(P, KD, SEQ).transpose(1, 0, 2).reshape(D_MODEL, SEQ).T)[None]
```
